# Optimizing a Trainium2 kernel written in Bass

```python
import jax, jax.numpy as jnp
from jax import lax
import numpy as np

D_MODEL = 2048
BATCH = 1
SEQ = 256
DEPTH = 2

N_MIXERS = 2
N_RET_LAYERS = (DEPTH + 1) // 2
N_NSA_LAYERS = DEPTH // 2
EPS = 1e-6
NEG_INF = -1e30
FORCE_SCORE = 1e4

RET_HEADS = 8
RET_DK = D_MODEL // RET_HEADS
RET_DV = 2 * RET_DK
RET_QK_W = RET_HEADS * RET_DK
RET_V_W = RET_HEADS * RET_DV
RET_IN = 2 * RET_QK_W + 2 * RET_V_W
RET_CHUNK = 128

NSA_HEADS = 16
NSA_GROUPS = 4
NSA_REP = NSA_HEADS // NSA_GROUPS
NSA_DH = D_MODEL // NSA_HEADS
NSA_WIDTH = NSA_HEADS * NSA_DH
NSA_KV = NSA_GROUPS * NSA_DH
NSA_BRANCHES = 3
NSA_IN = NSA_WIDTH + 6 * NSA_KV + NSA_HEADS * NSA_BRANCHES + NSA_WIDTH
CMP_LEN = 32
CMP_STRIDE = 16
SLC_BLOCK = 64
TOP_N = 16
WINDOW = 512
Q_BLOCK = 128

kernel_name = "interleaved_retention_nsa_gated_hybrid"

def rmsnorm(x, g):
    xf = x.astype(jnp.float32)
    y = xf * lax.rsqrt(jnp.mean(xf * xf, axis=-1, keepdims=True) + EPS)
    return (y * g.astype(jnp.float32)).astype(x.dtype)

def masked_softmax(s, mask):
    p = jax.nn.softmax(jnp.where(mask, s, NEG_INF), axis=-1)
    return jnp.where(mask, p, 0.0)

def alibi_slopes(n_heads):
    return jnp.exp2(-8.0 * jnp.arange(1, n_heads + 1, dtype=jnp.float32) / n_heads)

def retention_mixer(h, w_in, w_out):
    B, S, _ = h.shape
    H, C = RET_HEADS, RET_CHUNK
    n = S // C
    proj = h @ w_in
    q, k, v, gate = jnp.split(proj, [RET_QK_W, 2 * RET_QK_W, 2 * RET_QK_W + RET_V_W], axis=-1)

    def heads(t, d):
        return t.reshape(B, n, C, H, d).transpose(1, 0, 3, 2, 4).astype(jnp.float32)

    q = heads(q, RET_DK)
    k = heads(k, RET_DK) * (RET_DK ** -0.5)
    v = heads(v, RET_DV)
    log_g = jnp.log1p(-jnp.exp2(-5.0 - jnp.arange(H, dtype=jnp.float32)))
    idx = jnp.arange(C, dtype=jnp.float32)
    diff = idx[:, None] - idx[None, :]
    decay_intra = jnp.where(diff >= 0, jnp.exp(diff[None] * log_g[:, None, None]), 0.0)
    q_decay = jnp.exp((idx[None, :] + 1.0) * log_g[:, None])[None, :, :, None]
    k_decay = jnp.exp((C - 1.0 - idx[None, :]) * log_g[:, None])[None, :, :, None]
    chunk_decay = jnp.exp(C * log_g)[None, :, None, None]

    def step(state, qkv):
        qc, kc, vc = qkv
        scores = jnp.einsum('bhnd,bhmd->bhnm', qc, kc) * decay_intra
        o = (jnp.einsum('bhnm,bhmv->bhnv', scores, vc)
             + jnp.einsum('bhnd,bhdv->bhnv', qc, state) * q_decay)
        state = state * chunk_decay + jnp.einsum('bhmd,bhmv->bhdv', kc * k_decay, vc)
        return state, o

    state0 = jnp.zeros((B, H, RET_DK, RET_DV), jnp.float32)
    _, o = lax.scan(step, state0, (q, k, v))
    mu = jnp.mean(o, axis=-1, keepdims=True)
    var = jnp.mean(jnp.square(o - mu), axis=-1, keepdims=True)
    o = (o - mu) * lax.rsqrt(var + EPS)
    o = o.transpose(1, 0, 3, 2, 4).reshape(B, S, RET_V_W)
    y = jax.nn.silu(gate.astype(jnp.float32)) * o
    return y.astype(h.dtype) @ w_out

def compress_blocks(raw, pos, w1, w2, blk_idx):
    B = raw.shape[0]
    n_cmp = blk_idx.shape[0]
    blocks = raw[:, blk_idx] + pos[None, None, :, None, :]
    flat = blocks.transpose(0, 1, 3, 2, 4).reshape(B, n_cmp, NSA_GROUPS, CMP_LEN * NSA_DH)
    return jax.nn.silu(flat @ w1) @ w2

def nsa_mixer(h, w_in, cmp_pos_k, cmp_w1_k, cmp_w2_k, cmp_pos_v, cmp_w1_v, cmp_w2_v, w_out):
    B, S, _ = h.shape
    G, R, dh, QB = NSA_GROUPS, NSA_REP, NSA_DH, Q_BLOCK
    nq = S // QB
    sizes = [NSA_WIDTH] + [NSA_KV] * 6 + [NSA_HEADS * NSA_BRANCHES]
    offs = [int(o) for o in np.cumsum(sizes)]
    proj = h @ w_in
    q, kc_raw, vc_raw, ks, vs, kw, vw, g, z = jnp.split(proj, offs, axis=-1)
    q = q.reshape(B, S, G, R, dh) * (dh ** -0.5)
    kv = lambda t: t.reshape(B, S, G, dh)
    kc_raw, vc_raw, ks, vs, kw, vw = map(kv, (kc_raw, vc_raw, ks, vs, kw, vw))
    gates = jax.nn.sigmoid(g.astype(jnp.float32)).reshape(B, S, G, R, NSA_BRANCHES)
    slopes = alibi_slopes(NSA_HEADS).reshape(G, R)

    n_cmp = (S - CMP_LEN) // CMP_STRIDE + 1
    blk_idx = jnp.arange(n_cmp)[:, None] * CMP_STRIDE + jnp.arange(CMP_LEN)[None, :]
    k_cmp = compress_blocks(kc_raw, cmp_pos_k, cmp_w1_k, cmp_w2_k, blk_idx)
    v_cmp = compress_blocks(vc_raw, cmp_pos_v, cmp_w1_v, cmp_w2_v, blk_idx)
    cmp_end = blk_idx[:, -1]

    n_slc = S // SLC_BLOCK
    n_sel = min(TOP_N, n_slc)
    cstart = jnp.arange(n_cmp) * CMP_STRIDE
    sstart = jnp.arange(n_slc) * SLC_BLOCK
    overlap = ((cstart[:, None] < sstart[None, :] + SLC_BLOCK)
               & (cstart[:, None] + CMP_LEN > sstart[None, :])).astype(jnp.float32)
    k_blk = ks.reshape(B, n_slc, SLC_BLOCK, G, dh).transpose(0, 3, 1, 2, 4)
    v_blk = vs.reshape(B, n_slc, SLC_BLOCK, G, dh).transpose(0, 3, 1, 2, 4)
    b_i = jnp.arange(B)[:, None, None, None]
    g_i = jnp.arange(G)[None, None, :, None]
    jj = jnp.arange(n_slc)

    kw_p = jnp.pad(kw, ((0, 0), (WINDOW, 0), (0, 0), (0, 0)))
    vw_p = jnp.pad(vw, ((0, 0), (WINDOW, 0), (0, 0), (0, 0)))

    q_blocks = q.reshape(B, nq, QB, G, R, dh).transpose(1, 0, 2, 3, 4, 5)
    g_blocks = gates.reshape(B, nq, QB, G, R, NSA_BRANCHES).transpose(1, 0, 2, 3, 4, 5)

    def block_fn(args):
        qi, qb, gb = args
        q0 = qi * QB
        t = q0 + jnp.arange(QB)
        dc = t[:, None] - cmp_end[None, :]
        sc = (jnp.einsum('bqgrd,bcgd->bqgrc', qb, k_cmp).astype(jnp.float32)
              - slopes[None, None, :, :, None] * dc.astype(jnp.float32)[None, :, None, None, :])
        pc = masked_softmax(sc, (dc >= 0)[None, :, None, None, :])
        o_cmp = jnp.einsum('bqgrc,bcgd->bqgrd', pc, v_cmp)
        imp = jnp.einsum('bqgrc,cj->bqgj', pc, overlap)
        cur = (t // SLC_BLOCK)[:, None]
        forced = (jj[None, :] == 0) | (jj[None, :] == cur) | (jj[None, :] == cur - 1)
        blk_ok = sstart[None, :] <= t[:, None]
        score = jnp.where(forced[None, :, None, :], FORCE_SCORE,
                          jnp.where(blk_ok[None, :, None, :], imp, -1.0))
        _, sel = lax.top_k(score, n_sel)
        kb = k_blk[b_i, g_i, sel]
        vb = v_blk[b_i, g_i, sel]
        tok = sel[..., None] * SLC_BLOCK + jnp.arange(SLC_BLOCK)
        ds = (t[None, :, None, None, None] - tok)[:, :, :, None]
        ss = (jnp.einsum('bqgrd,bqgnkd->bqgrnk', qb, kb).astype(jnp.float32)
              - slopes[None, None, :, :, None, None] * ds.astype(jnp.float32))
        flat_shape = ss.shape[:4] + (n_sel * SLC_BLOCK,)
        ps = masked_softmax(ss.reshape(flat_shape),
                            jnp.broadcast_to(ds >= 0, ss.shape).reshape(flat_shape)).reshape(ss.shape)
        o_slc = jnp.einsum('bqgrnk,bqgnkd->bqgrd', ps, vb)
        kwb = lax.dynamic_slice_in_dim(kw_p, q0, QB + WINDOW, axis=1)
        vwb = lax.dynamic_slice_in_dim(vw_p, q0, QB + WINDOW, axis=1)
        kpos = q0 - WINDOW + jnp.arange(QB + WINDOW)
        dw = t[:, None] - kpos[None, :]
        mw = (dw >= 0) & (dw < WINDOW) & (kpos[None, :] >= 0)
        sw = (jnp.einsum('bqgrd,bkgd->bqgrk', qb, kwb).astype(jnp.float32)
              - slopes[None, None, :, :, None] * dw.astype(jnp.float32)[None, :, None, None, :])
        pw = masked_softmax(sw, mw[None, :, None, None, :])
        o_win = jnp.einsum('bqgrk,bkgd->bqgrd', pw, vwb)
        return gb[..., 0:1] * o_cmp + gb[..., 1:2] * o_slc + gb[..., 2:3] * o_win

    o = lax.map(block_fn, (jnp.arange(nq), q_blocks, g_blocks))
    o = o.transpose(1, 0, 2, 3, 4, 5).reshape(B, S, NSA_WIDTH)
    y = jax.nn.silu(z.astype(jnp.float32)) * o.astype(jnp.float32)
    return y.astype(h.dtype) @ w_out

def setup_inputs(seed: int = 0) -> dict:
    key = jax.random.key(seed)
    ks = jax.random.split(key, 14)
    nrm = lambda k, shape, scale: jax.random.normal(k, shape, jnp.float32) * scale
    return {
        "x": nrm(ks[0], (BATCH, SEQ, D_MODEL), 1.0),
        "norm_g": 1.0 + nrm(ks[1], (DEPTH, D_MODEL), 0.01),
        "ret_w_in": nrm(ks[2], (N_RET_LAYERS, D_MODEL, RET_IN), D_MODEL ** -0.5),
        "ret_w_out": nrm(ks[3], (N_RET_LAYERS, RET_V_W, D_MODEL), RET_V_W ** -0.5),
        "nsa_w_in": nrm(ks[4], (N_NSA_LAYERS, D_MODEL, NSA_IN), D_MODEL ** -0.5),
        "nsa_cmp_pos_k": nrm(ks[5], (N_NSA_LAYERS, CMP_LEN, NSA_DH), 0.1),
        "nsa_cmp_w1_k": nrm(ks[6], (N_NSA_LAYERS, CMP_LEN * NSA_DH, NSA_DH), (CMP_LEN * NSA_DH) ** -0.5),
        "nsa_cmp_w2_k": nrm(ks[7], (N_NSA_LAYERS, NSA_DH, NSA_DH), NSA_DH ** -0.5),
        "nsa_cmp_pos_v": nrm(ks[8], (N_NSA_LAYERS, CMP_LEN, NSA_DH), 0.1),
        "nsa_cmp_w1_v": nrm(ks[9], (N_NSA_LAYERS, CMP_LEN * NSA_DH, NSA_DH), (CMP_LEN * NSA_DH) ** -0.5),
        "nsa_cmp_w2_v": nrm(ks[10], (N_NSA_LAYERS, NSA_DH, NSA_DH), NSA_DH ** -0.5),
        "nsa_w_out": nrm(ks[11], (N_NSA_LAYERS, NSA_WIDTH, D_MODEL), NSA_WIDTH ** -0.5),
        "final_g": 1.0 + nrm(ks[12], (D_MODEL,), 0.01),
    }

def reference(x, norm_g, ret_w_in, ret_w_out, nsa_w_in, nsa_cmp_pos_k, nsa_cmp_w1_k, nsa_cmp_w2_k,
              nsa_cmp_pos_v, nsa_cmp_w1_v, nsa_cmp_w2_v, nsa_w_out, final_g):
    h = x
    for i in range(DEPTH):
        hn = rmsnorm(h, norm_g[i])
        j = i // N_MIXERS
        if i % N_MIXERS == 0:
            h = h + retention_mixer(hn, ret_w_in[j], ret_w_out[j])
        else:
            h = h + nsa_mixer(hn, nsa_w_in[j], nsa_cmp_pos_k[j], nsa_cmp_w1_k[j], nsa_cmp_w2_k[j],
                              nsa_cmp_pos_v[j], nsa_cmp_w1_v[j], nsa_cmp_w2_v[j], nsa_w_out[j])
    return rmsnorm(h, final_g)


_drawn_inputs = setup_inputs


def setup_inputs(seed=0):
    import zlib

    import numpy as np

    out = dict(_drawn_inputs(seed))
    spreads = {}
    factors = {'norm_g': 4.853, 'nsa_cmp_pos_k': 8.0, 'nsa_cmp_pos_v': 3.87, 'final_g': 5.806}
    for name, (base, spread) in spreads.items():
        noise = np.random.default_rng([zlib.crc32(name.encode()), seed]).standard_normal(out[name].shape)
        drawn = base * np.exp(spread * noise) if base else spread * noise
        out[name] = __import__('jax').numpy.asarray(drawn.astype(out[name].dtype))
    for name, factor in factors.items():
        out[name] = (out[name] * factor).astype(out[name].dtype)
    return out
```

```python
from contextlib import ExitStack

import concourse.bass as bass
from concourse import mybir

F32 = mybir.dt.float32
F32R = mybir.dt.float32r
ACT = mybir.ActivationFunctionType
ALU = mybir.AluOpType
AX = mybir.AxisListType

P = 128
EPS = 1e-6
COLS = 512
KPC = 4
RING = 4
BRANCHES = 3
CMP_LEN, CMP_STRIDE = 32, 16
RET_HEADS = 8
NSA_HEADS = 16


def trunk(nc, x, norm_g, ret_w_in, ret_w_out, nsa_w_in, cmp_pos_k, cmp_w1_k, cmp_w2_k, cmp_pos_v,
          cmp_w1_v, cmp_w2_v, nsa_w_out, final_g, identity, decay, neg_slopes, distance, distance_cmp,
          cmp_seen, out):
    _, S, D = x.shape
    TT = S // P
    KT = D // P
    H = RET_HEADS
    DK = D // H
    G = NSA_HEADS // 4
    R = NSA_HEADS // G
    DH = D // NSA_HEADS
    KV = G * DH
    NC = (S - CMP_LEN) // CMP_STRIDE + 1
    NG = NSA_HEADS * BRANCHES
    GATE_COL = D + 6 * KV
    Z_COL = GATE_COL + NG
    CG = D // COLS
    assert TT == 2 and DK == 256 and KV == COLS and R * DH == COLS and CG == RING == KPC == 4

    ret_in = ret_w_in[0].rearrange("(k p) n -> p k n", p=P)
    ret_out = ret_w_out[0].rearrange("(k p) n -> p k n", p=P)
    nsa_in = nsa_w_in[0].rearrange("(k p) n -> p k n", p=P)
    nsa_out = nsa_w_out[0].rearrange("(k p) n -> p k n", p=P)
    x_rows = x[0].rearrange("(t p) d -> p t d", p=P)
    out_rows = out[0].rearrange("(t p) d -> p t d", p=P)

    with ExitStack() as ctx:
        def sb(name, shape, dt=F32):
            return ctx.enter_context(nc.sbuf_tensor(name, shape, dt))

        def sem(name):
            return ctx.enter_context(nc.semaphore(name))

        w_raw = sb("w_raw", [P, RING, KPC, COLS])
        w_hi = sb("w_hi", [P, RING, KPC, COLS], F32R)
        w_lo = sb("w_lo", [P, RING, KPC, COLS], F32R)
        hT_hi = sb("hT_hi", [P, KT, S], F32R)
        hT_lo = sb("hT_lo", [P, KT, S], F32R)
        yT_hi = sb("yT_hi", [P, KPC, S], F32R)
        yT_lo = sb("yT_lo", [P, KPC, S], F32R)
        res = sb("res", [P, TT, D])
        stage = sb("stage", [P, TT, COLS])
        ksT = sb("ksT", [P, G, S])
        kwT = sb("kwT", [P, G, S])
        vs = sb("vs", [P, TT, KV])
        vw = sb("vw", [P, TT, KV])
        ident = sb("ident", [P, P])
        dist = sb("dist", [P, 3 * P])
        dist_c = sb("dist_c", [P, TT * NC])
        seen = sb("seen", [P, 1])
        slopes = sb("slopes", [P, NSA_HEADS])
        cols = sb("cols", [P, 96])
        gates = sb("gates", [P, TT, NG])
        kcmpT = sb("kcmpT", [P, G * NC])
        vcmp = sb("vcmp", [NC, G * DH])
        sumsq = sb("sumsq", [P, TT, CG])
        meansq = sb("meansq", [P, TT])
        rstd = sb("rstd", [P, 3, TT])
        minus_half = sb("minus_half", [P, TT])
        bn6 = sb("bn6", [P, TT, 6])
        mv = sb("mv", [P, TT, 2])
        eps = sb("eps", [P, TT])
        head_rstd = sb("head_rstd", [P, TT])
        negmax = sb("negmax", [P, TT, BRANCHES])
        sums = sb("sums", [P, TT, BRANCHES])
        factor = sb("factor", [P, TT, BRANCHES])

        arena = sb("arena", [P, 7584])

        def piece(at, *dims):
            n = 1
            for d in dims:
                n *= d
            v = arena[:, at:at + n]
            if len(dims) == 2:
                v = v.rearrange("p (a b) -> p a b", a=dims[0])
            if len(dims) == 3:
                v = v.rearrange("p (a b c) -> p a b c", a=dims[0], b=dims[1])
            return v

        decays = piece(0, H, 2 * P)
        v_sb = piece(2048, TT, COLS)
        silu_gate = piece(3072, TT, COLS)
        y_sb = piece(4096, TT, COLS)
        qT = piece(5120, 2, S)
        kT = piece(5632, 2, S)
        sT = piece(6144, 3 * P)
        w1 = piece(0, CMP_LEN, DH)
        rawT = piece(4096, G, S)
        window = piece(5120, CMP_LEN, G * NC)
        vw_row = vw[:, :, :].rearrange("p t n -> p (t n)")
        gate_w = vw_row[:, 0:KT * NG].rearrange("p (k n) -> p k n", k=KT)
        w2 = vw_row[:, KT * NG:KT * NG + DH]
        hidden = vw_row[:, KT * NG + DH:KT * NG + DH + G * NC]
        pT = piece(0, 2, 3, R * P)
        pTc = piece(3072, TT, R * P)
        silu_zT = piece(4096, R, S)
        qhT = piece(5120, R, S)
        prob = piece(6144, 2, 3 * P)
        v_now = piece(6912, 4, P)
        vc_now = arena[0:NC, 7424:7424 + DH]
        prob_c = piece(7552, TT, NC)
        y32 = qhT
        final_gain = piece(0, D)

        acc = [[ctx.enter_context(nc.psum_tensor(f"acc{a}{t}", [P, COLS], F32)) for t in range(TT)] for a in range(2)]
        side = [ctx.enter_context(nc.psum_tensor(f"side{i}", [P, COLS], F32)) for i in range(4)]

        raw_in = [sem(f"raw_in{s}") for s in range(RING)]
        hi_done, lo_done = sem("hi_done"), sem("lo_done")
        chunk_done = sem("chunk_done")
        acc_free = [sem("acc_free0"), sem("acc_free1")]
        x_in = [sem(f"x_in{j}") for j in range(CG)]
        const_in, cols_in, late_in = sem("const_in"), sem("cols_in"), sem("late_in")
        w1_in, w2_in, gain_in = sem("w1_in"), sem("w2_in"), sem("gain_in")
        stored = sem("stored")
        cols_psum, cols_ready = sem("cols_psum"), sem("cols_ready")
        hT_psum, hT_hi_done, hT_done = sem("hT_psum"), sem("hT_hi_done"), sem("hT_done")
        squares_done, meansq_done, rstd_step, rstd_done = sem("squares_done"), sem("meansq_done"), sem("rstd_step"), sem("rstd_done")
        const_made = sem("const_made")
        qkT_psum, qT_ready, kT_ready = sem("qkT_psum"), sem("qT_ready"), sem("kT_ready")
        sT_psum, sT_ready, o_psum = sem("sT_psum"), sem("sT_ready"), sem("o_psum")
        stats_done, mv_done, head_rstd_step, head_rstd_done = sem("stats_done"), sem("mv_done"), sem("head_rstd_step"), sem("head_rstd_done")
        y0_ready, y_ready = sem("y0_ready"), sem("y_ready")
        yT_psum, yT_hi_done, yT_done = sem("yT_psum"), sem("yT_hi_done"), sem("yT_done")
        rawT_psum, rawT_ready = sem("rawT_psum"), sem("rawT_ready")
        window_ready, hid_psum, hid_ready, cmp_psum, cmp_ready = sem("window_ready"), sem("hid_psum"), sem("hid_ready"), sem("cmp_psum"), sem("cmp_ready")
        gw_hi, gw_done, gates_psum, gates_ready = sem("gw_hi"), sem("gw_done"), sem("gates_psum"), sem("gates_ready")
        qh_psum, qh_ready = sem("qh_psum"), sem("qh_ready")
        score_psum, score_read, negmax_ready, exp_done = sem("score_psum"), sem("score_read"), sem("negmax_ready"), sem("exp_done")
        recip_done, factor_done, prob_ready = sem("recip_done"), sem("factor_done"), sem("prob_ready")
        pT_psum, pT_ready, v_now_ready, pv_psum = sem("pT_psum"), sem("pT_ready"), sem("v_now_ready"), sem("pv_psum")
        zT_psum, zT_ready = sem("zT_psum"), sem("zT_ready")
        y32_done, nsa_hi_done, nsa_yT_done = sem("y32_done"), sem("nsa_hi_done"), sem("nsa_yT_done")
        final_done = sem("final_done")

        RET_C, NSA_C = 16, 12

        def ret_q(h):
            return 4 * h - 1 if not (type(h) is int and h == 0) else 0
        RET_TAIL_Q = 4 * H - 1
        KV_Q = RET_TAIL_Q + 1

        def nsa_q(g):
            return KV_Q + 6 + 3 * g - 1 if not (type(g) is int and g == 0) else KV_Q + 6
        NSA_TAIL_Q = KV_Q + 6 + 3 * G - 1
        LAST = 4 * NSA_TAIL_Q + 3

        def ret_uses(h):
            return (4 * h - 2, 3 * h - 2) if not (type(h) is int and h == 0) else (0, 0)
        RET_TAIL_USES = (4 * H - 2, 3 * H - 2)
        KV_USES = (RET_TAIL_USES[0] + 2, RET_TAIL_USES[1] + 2)
        NSA_USES = (KV_USES[0] + 3, KV_USES[1] + 4)

        def nsa_uses(g):
            first = type(g) is int and g == 0
            return tuple(u if first else u + 3 * g - 2 for u in NSA_USES)

        def added(n, j):
            pair = (j + n) % 2
            return acc_free[pair], (RET_TAIL_USES if n == 1 else nsa_uses(G))[pair] + j // 2 + 1

        block = ctx.enter_context(nc.Block())

        @block.sync
        def _(sp):
            def chunk(q, s, halves):
                if not (type(q) is int and q == 0):
                    sp.wait_ge(lo_done, 4 * q + s - 3)
                for to, src in halves:
                    sp.dma_start(to, src).then_inc(raw_in[s], 16)

            def by_rows(s, w, k0, col):
                return [(w_raw[:, s, 2 * i:2 * i + 2, :], w[:, bass.ds(k0 + 2 * i, 2), bass.ds(col, COLS)]) for i in range(2)]

            def by_columns(s, w, k0, col_a, col_b):
                return [(w_raw[:, s, :, i * DK:(i + 1) * DK], w[:, k0:k0 + KPC, bass.ds(c, DK)]) for i, c in enumerate((col_a, col_b))]

            def ret_inputs(h):
                q = ret_q(h)
                for c in range(12):
                    s = c % RING
                    if c < 4:
                        chunk(q, s, by_columns(s, ret_in, KPC * s, h * DK, D + h * DK))
                    elif c < 8:
                        chunk(q + 1, s, by_rows(s, ret_in, KPC * s, 2 * D + h * COLS))
                    else:
                        chunk(q + 2, s, by_rows(s, ret_in, KPC * s, 4 * D + h * COLS))

            def outputs(q, w, head):
                for j in range(CG):
                    chunk(q, j, by_rows(j, w, head * KPC, j * COLS))

            for j in range(CG):
                sp.dma_start(res[:, :, j * COLS:(j + 1) * COLS], x_rows[:, :, j * COLS:(j + 1) * COLS]).then_inc(x_in[j], 16)
            ret_inputs(0)
            with sp.Fori(1, H) as h:
                ret_inputs(h)
                outputs(ret_q(h) + 3, ret_out, h - 1)
            outputs(RET_TAIL_Q, ret_out, H - 1)
            for i in range(6):
                for s in range(RING):
                    chunk(KV_Q + i, s, by_rows(s, nsa_in, KPC * s, D + i * KV))

            def nsa_inputs(g):
                for s in range(RING):
                    chunk(nsa_q(g), s, by_rows(s, nsa_in, KPC * s, g * COLS))
                for s in range(RING):
                    chunk(nsa_q(g) + 1, s, by_rows(s, nsa_in, KPC * s, Z_COL + g * COLS))

            nsa_inputs(0)
            with sp.Fori(1, G) as g:
                nsa_inputs(g)
                outputs(nsa_q(g) + 2, nsa_out, g - 1)
            outputs(NSA_TAIL_Q, nsa_out, G - 1)
            for t in range(TT):
                for i in range(2):
                    sp.wait_ge(final_done, 2 * t + i + 1)
                    sp.dma_start(out_rows[:, t, i * D // 2:(i + 1) * D // 2], res[:, t, i * D // 2:(i + 1) * D // 2]).then_inc(stored, 16)
            sp.wait_ge(stored, 16 * 2 * TT)

        @block.gpsimd
        def _(pool):
            pool.dma_start(ident[:, :], identity).then_inc(cols_in, 16)
            pool.dma_start(stage[0:2 * KT, 0, 0:P], norm_g.rearrange("l (k p) -> (l k) p", p=P)).then_inc(cols_in, 16)
            pool.dma_start(stage[2 * KT:2 * KT + CMP_LEN, 0, 0:P], cmp_pos_k[0]).then_inc(cols_in, 16)
            pool.dma_start(stage[2 * KT + CMP_LEN:96, 0, 0:P], cmp_pos_v[0]).then_inc(cols_in, 16)
            pool.dma_start(decays, decay).then_inc(const_in, 16)
            pool.dma_start(slopes[:, :], neg_slopes).then_inc(late_in, 16)
            pool.dma_start(dist[:, :], distance).then_inc(late_in, 16)
            pool.dma_start(dist_c[:, :], distance_cmp).then_inc(late_in, 16)
            pool.dma_start(seen[:, :], cmp_seen).then_inc(late_in, 16)
            pool.memset(minus_half[:, :], -0.5).then_inc(const_made, 1)
            pool.wait_ge(const_made, 1)

            def token_factor(n):
                pool.wait_ge(meansq_done, n + 1)
                pool.tensor_scalar(meansq[:, :], meansq[:, :], 1.0 / D, EPS, ALU.mult, ALU.add).then_inc(rstd_step, 1)
                pool.wait_ge(rstd_step, n + 1)
                pool.tensor_tensor(rstd[:, n, :], meansq[:, :], minus_half[:, :], ALU.pow).then_inc(rstd_done, 1)

            def head_factor(h):
                pool.wait_ge(mv_done, TT * h + TT)
                pool.tensor_tensor(head_rstd[:, :], mv[:, :, 1], eps[:, :], ALU.add).then_inc(head_rstd_step, 1)
                pool.wait_ge(head_rstd_step, h + 1)
                pool.tensor_tensor(head_rstd[:, :], head_rstd[:, :], minus_half[:, :], ALU.pow).then_inc(head_rstd_done, 1)

            token_factor(0)
            head_factor(0)
            with pool.Fori(1, H) as h:
                head_factor(h)
            pool.wait_ge(yT_done, H)
            pool.dma_start(w1, cmp_w1_k[0].rearrange("(l d) n -> d l n", d=DH)).then_inc(w1_in, 16)
            pool.dma_start(w2[:, :], cmp_w2_k[0]).then_inc(w2_in, 16)
            pool.dma_start(gate_w, nsa_in[:, :, GATE_COL:GATE_COL + NG]).then_inc(w1_in, 16)
            token_factor(1)
            pool.wait_ge(hid_psum, 1)
            pool.dma_start(w1, cmp_w1_v[0].rearrange("(l d) n -> d l n", d=DH)).then_inc(w1_in, 16)
            pool.wait_ge(cmp_psum, 1)
            pool.dma_start(w2[:, :], cmp_w2_v[0]).then_inc(w2_in, 16)

            def group_values(g):
                if not (type(g) is int and g == 0):
                    pool.wait_ge(pv_psum, g)
                for b, v in enumerate((vs, vw)):
                    pool.tensor_copy(v_now[:, 2 * b:2 * b + 2, :], v[:, :, bass.ds(g * DH, DH)])
                pool.tensor_copy(vc_now[:, :], vcmp[:, bass.ds(g * DH, DH)]).then_inc(v_now_ready, 1)

            pool.wait_ge(gates_ready, 1)
            pool.wait_ge(cmp_ready, 2)
            group_values(0)
            with pool.Fori(1, G) as g:
                group_values(g)
            pool.wait_ge(pv_psum, G)
            pool.dma_start(final_gain, final_g.rearrange("(o d) -> o d", o=1).to_broadcast([P, D])).then_inc(gain_in, 16)
            token_factor(2)
            pool.wait_ge(stored, 16 * 2 * TT)

        @block.scalar
        def _(act):
            def high(q, s):
                act.wait_ge(raw_in[s], 32 * q + 32)
                if not (type(q) is int and q == 0):
                    act.wait_ge(chunk_done, 4 * q + s - 3)
                act.copy(w_hi[:, s, :, :], w_raw[:, s, :, :]).then_inc(hi_done, 1)

            def ahead(q, c):
                high(q + (c + 2) // RING, (c + 2) % RING)

            def norm_high(layer, j):
                act.wait_ge(hT_psum, CG * layer + j + 1)
                if layer == 0 and j == 0:
                    act.wait_ge(cols_ready, 1)
                for i in range(KPC):
                    k = KPC * j + i
                    ins = act.activation(hT_hi[:, k, :], side[2 * (j % 2) + i // 2][:, (i % 2) * S:(i % 2 + 1) * S], ACT.Copy,
                                         scale=cols[:, KT * layer + k:KT * layer + k + 1])
                ins.then_inc(hT_hi_done, 1)

            def squares(n, j):
                if n == 0:
                    act.wait_ge(x_in[j], 16)
                    act.wait_ge(cols_psum, 1)
                else:
                    act.wait_ge(*added(n, j))
                if n or j:
                    act.wait_ge(squares_done, CG * n + j)
                for t in range(TT):
                    ins = act.activation(stage[:, t, :], res[:, t, j * COLS:(j + 1) * COLS], ACT.Square, accum_out=sumsq[:, t, j:j + 1])
                ins.then_inc(squares_done, 1)

            norm_high(0, 0)
            high(0, 0)
            norm_high(0, 1)
            high(0, 1)

            def retention(h):
                first = type(h) is int and h == 0
                q = ret_q(h)
                n0 = 4 * q
                for c in range(12 if first else RET_C):
                    ahead(q, c)
                    if first and c < 2:
                        norm_high(0, 2 + c)
                    if first and c == 1:
                        for j in range(CG):
                            squares(0, j)
                    if c == 4:
                        act.wait_ge(qkT_psum, h + 1)
                        act.copy(qT, side[0][:, :].rearrange("p (a b) -> p a b", a=2)).then_inc(qT_ready, 1)
                    if c == 7:
                        act.wait_ge(chunk_done, n0 + 8)
                        for t in range(TT):
                            ins = act.activation(v_sb[:, t, :], acc[1][t][:, :], ACT.Copy, scale=rstd[:, 0, t:t + 1])
                        ins.then_inc(acc_free[1], 1)
                    if c == 11:
                        act.wait_ge(chunk_done, n0 + 12)
                        for t in range(TT):
                            ins = act.activation(silu_gate[:, t, :], acc[0][t][:, :], ACT.Silu, scale=rstd[:, 0, t:t + 1])
                        ins.then_inc(acc_free[0], 1)
                    if c == (11 if first else 12):
                        act.wait_ge(y0_ready, h + 1)
                        act.wait_ge(head_rstd_done, h + 1)
                        for t in range(TT):
                            ins = act.activation(y_sb[:, t, :], y_sb[:, t, :], ACT.Copy, scale=head_rstd[:, t:t + 1])
                        ins.then_inc(y_ready, 1)
                    if c == (11 if first else 15):
                        act.wait_ge(yT_psum, h + 1)
                        for i in range(2):
                            act.copy(yT_hi[:, 2 * i:2 * i + 2, :], side[2 + i][:, :].rearrange("p (a b) -> p a b", a=2)).then_inc(yT_hi_done, 1)

            retention(0)
            with act.Fori(1, H) as h:
                retention(h)
            for j in range(CG):
                ahead(RET_TAIL_Q, j)
                if j:
                    norm_high(1, j - 1)
                squares(1, j)

            def compress(i, bank):
                act.wait_ge(hid_psum, i + 1)
                act.activation(hidden[:, :], side[bank][:, 0:G * NC], ACT.Silu).then_inc(hid_ready, 1)

            for c in range(24):
                ahead(KV_Q, c)
                if c == 0:
                    norm_high(1, 3)
                if c in (4, 8, 12, 20):
                    n = (4, 8, 12, 20).index(c)
                    to = (rawT, rawT, ksT[:, :, :], kwT[:, :, :])[n]
                    act.wait_ge(rawT_psum, n + 1)
                    if n == 1:
                        act.wait_ge(window_ready, 1)
                    for i in range(2):
                        ins = act.copy(to[:, 2 * i:2 * i + 2, :], side[i][:, :].rearrange("p (a b) -> p a b", a=2))
                    ins.then_inc(rawT_ready, 1)
                if c in (5, 9):
                    compress(0 if c == 5 else 1, 2)
                if c in (6, 10):
                    n = 0 if c == 6 else 1
                    act.wait_ge(cmp_psum, n + 1)
                    if n == 0:
                        act.copy(kcmpT[:, :], side[3][:, 0:G * NC]).then_inc(cmp_ready, 1)
                    else:
                        act.copy(vcmp[:, :], side[3][0:NC, :]).then_inc(cmp_ready, 1)
                if c == 16:
                    act.wait_ge(w1_in, 32)
                    act.copy(yT_hi[:, 0:3, :].rearrange("p a b -> p (a b)"), gate_w.rearrange("p a b -> p (a b)")).then_inc(gw_hi, 1)
                if c == 23:
                    act.wait_ge(gates_psum, 1)
                    for t in range(TT):
                        ins = act.activation(gates[:, t, :], acc[1][t][:, 0:NG], ACT.Sigmoid, scale=rstd[:, 1, t:t + 1])
                    ins.then_inc(acc_free[1], 1)

            def head_exps(g, r):
                u = R * g + r
                act.wait_ge(negmax_ready, u + 1)
                for b in range(2):
                    for t, (a, z) in enumerate(((0, P), (P, 3 * P))):
                        act.activation(prob[:, b, a:z], prob[:, b, a:z], ACT.Exp, bias=negmax[:, t, b + 1:b + 2],
                                       accum_out=sums[:, t, b + 1:b + 2])
                for t in range(TT):
                    ins = act.activation(prob_c[:, t, :], prob_c[:, t, :], ACT.Exp, bias=negmax[:, t, 0:1], accum_out=sums[:, t, 0:1])
                ins.then_inc(exp_done, 1)

            def take_pT(g, r):
                act.wait_ge(pT_psum, R * g + r + 1)
                for b in range(2):
                    act.copy(pT[:, b, :, r * P:(r + 1) * P], side[b][:, 0:3 * P].rearrange("p (a b) -> p a b", a=3))
                    ins = act.copy(pTc[0:NC, b, r * P:(r + 1) * P], side[b][0:NC, 3 * P:4 * P])
                ins.then_inc(pT_ready, 1)

            def take_z(q):
                act.wait_ge(chunk_done, 4 * q + 8)
                for t in range(TT):
                    ins = act.activation(stage[:, t, :], acc[1][t][:, :], ACT.Silu, scale=rstd[:, 1, t:t + 1])
                ins.then_inc(acc_free[1], 1)

            def take_zT(g):
                act.wait_ge(zT_psum, g + 1)
                for i in range(2):
                    ins = act.copy(silu_zT[:, 2 * i:2 * i + 2, :], side[i][:, :].rearrange("p (a b) -> p a b", a=2))
                ins.then_inc(zT_ready, 1)

            def high_y(g):
                act.wait_ge(y32_done, g + 1)
                act.copy(yT_hi[:, :, :], y32).then_inc(nsa_hi_done, 1)

            def sparse(g):
                first = type(g) is int and g == 0
                q = nsa_q(g)
                for c in range(8 if first else NSA_C):
                    ahead(q, c)
                    if c == 4:
                        act.wait_ge(qh_psum, g + 1)
                        for i in range(2):
                            ins = act.activation(qhT[:, 2 * i:2 * i + 2, :], side[i][:, :].rearrange("p (a b) -> p a b", a=2), ACT.Copy, scale=float(DH) ** -0.5)
                        ins.then_inc(qh_ready, 1)
                    if c == 7:
                        take_z(q)
                    if not first:
                        if 5 <= c <= 8:
                            head_exps(g, c - 5)
                        if 6 <= c <= 9:
                            take_pT(g, c - 6)
                        if c == 10:
                            take_zT(g)
                        if c == 11:
                            high_y(g)
                    elif c == 7:
                        for r in range(R):
                            head_exps(g, r)
                            take_pT(g, r)
                        take_zT(g)
                        high_y(g)

            sparse(0)
            with act.Fori(1, G) as g:
                sparse(g)
            for j in range(CG):
                if j < 2:
                    ahead(NSA_TAIL_Q, j)
                squares(2, j)

        @block.vector
        def _(dve):
            def low(q, s):
                dve.wait_ge(hi_done, 4 * q + s + 1)
                dve.tensor_tensor(w_lo[:, s, :, :], w_raw[:, s, :, :], w_hi[:, s, :, :].bitcast(F32), ALU.subtract).then_inc(lo_done, 1)

            def ahead(q, c):
                low(q + (c + 2) // RING, (c + 2) % RING)

            def norm_low(layer, j):
                dve.wait_ge(hT_hi_done, CG * layer + j + 1)
                for i in range(KPC):
                    k = KPC * j + i
                    ins = dve.scalar_tensor_tensor(out=hT_lo[:, k, :], in0=side[2 * (j % 2) + i // 2][:, (i % 2) * S:(i % 2 + 1) * S],
                                                   scalar=cols[:, KT * layer + k:KT * layer + k + 1], in1=hT_hi[:, k, :].bitcast(F32),
                                                   op0=ALU.mult, op1=ALU.subtract)
                ins.then_inc(hT_done, 1)

            def mean_square(n):
                dve.wait_ge(squares_done, CG * n + CG)
                if n:
                    dve.wait_ge(rstd_done, n)
                dve.tensor_reduce(meansq[:, :], sumsq[:, :, :], AX.X, ALU.add).then_inc(meansq_done, 1)

            def add_residual(chunk, pair, j):
                dve.wait_ge(chunk_done, chunk + 1)
                for t in range(TT):
                    at = res[:, t, j * COLS:(j + 1) * COLS]
                    ins = dve.tensor_tensor(at, acc[pair][t][:, :], at, ALU.add)
                ins.then_inc(acc_free[pair], 1)

            def take(chunk, pair, to, layer):
                dve.wait_ge(chunk_done, chunk)
                dve.wait_ge(rstd_done, layer + 1)
                for t in range(TT):
                    ins = dve.tensor_scalar(to[:, t, :], acc[pair][t][:, :], rstd[:, layer, t:t + 1], None, ALU.mult)
                ins.then_inc(acc_free[pair], 1)

            dve.wait_ge(cols_psum, 1)
            dve.tensor_copy(cols[:, :], acc[1][0][:, 0:96]).then_inc(cols_ready, 1)
            dve.wait_ge(cols_ready, 1)
            norm_low(0, 0)
            low(0, 0)
            norm_low(0, 1)
            low(0, 1)

            def head_stats(h):
                dve.wait_ge(o_psum, h + 1)
                for t in range(TT):
                    dve.bn_stats(bn6[:, t, :], side[t][:, :]).then_inc(stats_done, 1)
                dve.wait_ge(stats_done, TT * h + TT)
                dve.memset(eps[:, :], EPS)
                for t in range(TT):
                    dve.bn_aggr(mv[:, t, :], bn6[:, t, :]).then_inc(mv_done, 1)

            def head_y(h):
                dve.wait_ge(acc_free[0], ret_uses(h)[0] + 2)
                dve.wait_ge(mv_done, TT * h + TT)
                for t in range(TT):
                    ins = dve.scalar_tensor_tensor(out=y_sb[:, t, :], in0=side[t][:, :], scalar=mv[:, t, 0:1], in1=silu_gate[:, t, :],
                                                   op0=ALU.subtract, op1=ALU.mult)
                ins.then_inc(y0_ready, 1)

            def low_yT(h):
                for i in range(2):
                    dve.wait_ge(yT_hi_done, 2 * h + i + 1)
                    ins = dve.tensor_tensor(yT_lo[:, 2 * i:2 * i + 2, :], side[2 + i][:, :].rearrange("p (a b) -> p a b", a=2),
                                            yT_hi[:, 2 * i:2 * i + 2, :].bitcast(F32), ALU.subtract)
                ins.then_inc(yT_done, 1)

            def retention(h):
                first = type(h) is int and h == 0
                q = ret_q(h)
                for c in range(12 if first else RET_C):
                    ahead(q, c)
                    if first and c < 2:
                        norm_low(0, 2 + c)
                    if first and c == 1:
                        mean_square(0)
                    if c == 3:
                        take(4 * q + 4, 0, stage, 0)
                    if c == 4:
                        dve.wait_ge(qkT_psum, h + 1)
                        dve.tensor_copy(kT, side[1][:, :].rearrange("p (a b) -> p a b", a=2)).then_inc(kT_ready, 1)
                    if c == 5:
                        dve.wait_ge(sT_psum, h + 1)
                        if first:
                            dve.wait_ge(const_in, 16)
                        mask = decays[:, bass.ds(h, 1), :].rearrange("p a b -> p (a b)")
                        dve.tensor_tensor(sT[:, 0:2 * P], side[2][:, 0:2 * P], mask, ALU.mult)
                        dve.tensor_tensor(sT[:, 2 * P:3 * P], side[2][:, 2 * P:3 * P], mask[:, 0:P], ALU.mult).then_inc(sT_ready, 1)
                    if c == 8:
                        head_stats(h)
                    if c == (11 if first else 12):
                        head_y(h)
                    if c >= 12:
                        j = c - 12
                        add_residual(4 * q + c, (j + 1) % 2, j)
                    if c == (11 if first else 15):
                        low_yT(h)

            retention(0)
            with dve.Fori(1, H) as h:
                retention(h)
            for j in range(CG):
                ahead(RET_TAIL_Q, j)
                add_residual(4 * RET_TAIL_Q + j, (j + 1) % 2, j)
                if j:
                    norm_low(1, j - 1)

            def make_window(n):
                dve.wait_ge(rawT_ready, n + 1)
                if n:
                    dve.wait_ge(hid_psum, n)
                pos = cols[:, 2 * KT + CMP_LEN * n:2 * KT + CMP_LEN * (n + 1)]
                for g in range(G):
                    base = rawT[:, g, 0:CMP_LEN]
                    raw_at = bass.AP(base.tensor, base.offset, [base.ap[0], [1, CMP_LEN], [CMP_STRIDE, NC]])
                    pos_at = bass.AP(pos.tensor, pos.offset, [pos.ap[0], [1, CMP_LEN], [0, NC]])
                    ins = dve.tensor_tensor(window[:, :, g * NC:(g + 1) * NC], raw_at, pos_at, ALU.add)
                ins.then_inc(window_ready, 1)

            for c in range(24):
                ahead(KV_Q, c)
                if c == 0:
                    norm_low(1, 3)
                if c == 1:
                    mean_square(1)
                n = 4 * KV_Q + c + 1
                if c in (3, 7, 11, 19):
                    take(n, (c // 4 + 1) % 2, stage, 1)
                if c in (4, 8):
                    make_window(c // 4 - 1)
                if c == 15:
                    take(n, 0, vs, 1)
                if c == 17:
                    dve.wait_ge(gw_hi, 1)
                    dve.tensor_tensor(yT_lo[:, 0:3, :].rearrange("p a b -> p (a b)"), gate_w.rearrange("p a b -> p (a b)"),
                                      yT_hi[:, 0:3, :].rearrange("p a b -> p (a b)").bitcast(F32), ALU.subtract).then_inc(gw_done, 1)
                if c == 23:
                    take(n, 0, vw, 1)
                    dve.wait_ge(acc_free[1], NSA_USES[1])
                    dve.wait_ge(late_in, 64)
                    cmp_gates = gates[:, 0, 0:NG:BRANCHES]
                    dve.tensor_scalar(cmp_gates, cmp_gates, seen[:, 0:1], None, ALU.mult).then_inc(gates_ready, 1)

            def head_scores(g, r):
                u = R * g + r
                dve.wait_ge(score_psum, u + 1)
                slope = slopes[:, bass.ds(g * R + r, 1)]
                for b in range(2):
                    dve.scalar_tensor_tensor(out=prob[:, b, :], in0=dist[:, :], scalar=slope, in1=side[2 + b][:, 0:3 * P],
                                             op0=ALU.mult, op1=ALU.add)
                dve.scalar_tensor_tensor(out=prob_c.rearrange("p a b -> p (a b)"), in0=dist_c[:, :], scalar=slope,
                                         in1=side[2][:, 3 * P:3 * P + TT * NC], op0=ALU.mult, op1=ALU.add).then_inc(score_read, 1)
                dve.wait_ge(score_read, u + 1)
                dve.tensor_reduce(negmax[:, 0, 1:3], prob[:, :, 0:P], AX.X, ALU.max, negate=True)
                dve.tensor_reduce(negmax[:, 1, 1:3], prob[:, :, P:3 * P], AX.X, ALU.max, negate=True)
                dve.tensor_reduce(negmax[:, :, 0], prob_c[:, :, :], AX.X, ALU.max, negate=True).then_inc(negmax_ready, 1)

            def head_probs(g, r):
                u = R * g + r
                dve.wait_ge(exp_done, u + 1)
                dve.reciprocal(sums[:, :, :], sums[:, :, :]).then_inc(recip_done, 1)
                dve.wait_ge(recip_done, u + 1)
                dve.tensor_tensor(factor[:, :, :], sums[:, :, :], gates[:, :, bass.ds(g * R * BRANCHES + r * BRANCHES, BRANCHES)], ALU.mult).then_inc(factor_done, 1)
                dve.wait_ge(factor_done, u + 1)
                for b in range(2):
                    for t, (a, z) in enumerate(((0, P), (P, 3 * P))):
                        dve.tensor_scalar(prob[:, b, a:z], prob[:, b, a:z], factor[:, t, b + 1:b + 2], None, ALU.mult)
                for t in range(TT):
                    ins = dve.tensor_scalar(prob_c[:, t, :], prob_c[:, t, :], factor[:, t, 0:1], None, ALU.mult)
                ins.then_inc(prob_ready, 1)

            def combine(g):
                dve.wait_ge(zT_ready, g + 1)
                dve.wait_ge(pv_psum, g + 1)
                for t in range(TT):
                    ins = dve.tensor_tensor(y32[:, :, t * P:(t + 1) * P], side[2 + t][:, :].rearrange("p (a b) -> p a b", a=R),
                                            silu_zT[:, :, t * P:(t + 1) * P], ALU.mult)
                ins.then_inc(y32_done, 1)

            def low_y(g):
                dve.wait_ge(nsa_hi_done, g + 1)
                dve.tensor_tensor(yT_lo[:, :, :], y32, yT_hi[:, :, :].bitcast(F32), ALU.subtract).then_inc(nsa_yT_done, 1)

            def sparse(g):
                first = type(g) is int and g == 0
                q = nsa_q(g)
                for c in range(8 if first else NSA_C):
                    ahead(q, c)
                    if c == 3:
                        take(4 * q + 4, 0, stage, 1)
                    if c >= 8:
                        add_residual(4 * q + c, c % 2, c - 8)
                    if not first:
                        if 5 <= c <= 8:
                            head_scores(g, c - 5)
                            head_probs(g, c - 5)
                        if c == 11:
                            combine(g)
                            low_y(g)
                    elif c == 7:
                        for r in range(R):
                            head_scores(g, r)
                            head_probs(g, r)
                        combine(g)
                        low_y(g)

            sparse(0)
            with dve.Fori(1, G) as g:
                sparse(g)
            for j in range(CG):
                if j < 2:
                    ahead(NSA_TAIL_Q, j)
                add_residual(4 * NSA_TAIL_Q + j, j % 2, j)
            mean_square(2)
            dve.wait_ge(rstd_done, 3)
            dve.wait_ge(gain_in, 16)
            for t in range(TT):
                for i in range(2):
                    half = slice(i * D // 2, (i + 1) * D // 2)
                    dve.scalar_tensor_tensor(out=res[:, t, half], in0=res[:, t, half], scalar=rstd[:, 2, t:t + 1],
                                             in1=final_gain[:, half], op0=ALU.mult, op1=ALU.mult).then_inc(final_done, 1)

        @block.tensor
        def _(pe):
            def chunk(q, s, xT_hi, xT_lo, k0, pair, start, stop):
                n = 4 * q + s
                pe.wait_ge(lo_done, n + 1)
                for t in range(TT):
                    tok = slice(t * P, (t + 1) * P)
                    for i in range(KPC):
                        a, z = start and i == 0, stop and i == KPC - 1
                        o = acc[pair][t][:, :]
                        pe.matmul(o, xT_hi[:, k0 + i, tok], w_hi[:, s, i, :], start=a, stop=False)
                        pe.matmul(o, xT_hi[:, k0 + i, tok], w_lo[:, s, i, :], start=False, stop=False)
                        ins = pe.matmul(o, xT_lo[:, k0 + i, tok], w_hi[:, s, i, :], start=False, stop=z)
                ins.then_inc(chunk_done, 1)

            def in_chunk(q, c, pair, uses):
                s = c % RING
                if s == 0 and not (type(uses) is int and uses == 0):
                    pe.wait_ge(acc_free[pair], uses)
                chunk(q, s, hT_hi, hT_lo, KPC * s, pair, s == 0, s == RING - 1)

            def out_chunk(q, j, pair, uses):
                pe.wait_ge(acc_free[pair], uses)
                chunk(q, j, yT_hi, yT_lo, 0, pair, True, True)

            def transpose_norm(layer, j):
                if layer == 0:
                    pe.wait_ge(x_in[j], 16)
                else:
                    pe.wait_ge(*added(1, j))
                if j >= 2:
                    pe.wait_ge(hT_done, CG * layer + j - 1)
                for i in range(KPC):
                    k = KPC * j + i
                    for t in range(TT):
                        at = (i % 2) * S + t * P
                        ins = pe.transpose(side[2 * (j % 2) + i // 2][:, at:at + P], res[:, t, k * P:(k + 1) * P], ident[:, :])
                ins.then_inc(hT_psum, 1)

            def transpose_tiles(src, banks):
                for i in range(4):
                    for t in range(TT):
                        at = (i % 2) * S + t * P
                        ins = pe.transpose(side[banks[i // 2]][:, at:at + P], src[:, t, i * P:(i + 1) * P], ident[:, :])
                return ins

            pe.wait_ge(cols_in, 64)
            pe.transpose(acc[1][0][:, 0:96], stage[0:96, 0, 0:P], ident[0:96, 0:96]).then_inc(cols_psum, 1)
            transpose_norm(0, 0)
            transpose_norm(0, 1)

            def retention(h):
                first = type(h) is int and h == 0
                q = ret_q(h)
                u0, u1 = ret_uses(h)
                for c in range(12):
                    if first and c < 4:
                        pe.wait_ge(hT_done, c + 1)
                    in_chunk(q + c // 4, c, (0, 1, 0)[c // 4], (u0, u1, u0 + 1)[c // 4])
                    if first and c < 2:
                        transpose_norm(0, 2 + c)
                    if c == 4:
                        pe.wait_ge(acc_free[0], u0 + 1)
                        if not first:
                            pe.wait_ge(y0_ready, h)
                        transpose_tiles(stage, (0, 1)).then_inc(qkT_psum, 1)
                    if c == 5:
                        pe.wait_ge(qT_ready, h + 1)
                        pe.wait_ge(kT_ready, h + 1)
                        if not first:
                            pe.wait_ge(yT_done, h)
                        else:
                            pe.wait_ge(hT_done, CG)
                        for i in range(2):
                            pe.matmul(side[2][:, 0:2 * P], kT[:, i, 0:P], qT[:, i, :], start=(i == 0), stop=(i == 1))
                        for i in range(2):
                            ins = pe.matmul(side[2][:, 2 * P:3 * P], kT[:, i, P:2 * P], qT[:, i, P:2 * P], start=(i == 0), stop=(i == 1))
                        ins.then_inc(sT_psum, 1)
                    if c == 8:
                        pe.wait_ge(sT_ready, h + 1)
                        pe.wait_ge(acc_free[1], u1 + 1)
                        pe.matmul(side[0][:, :], sT[:, 0:P], v_sb[:, 0, :], start=True, stop=True)
                        pe.matmul(side[1][:, :], sT[:, P:2 * P], v_sb[:, 0, :], start=True, stop=False)
                        pe.matmul(side[1][:, :], sT[:, 2 * P:3 * P], v_sb[:, 1, :], start=False, stop=True).then_inc(o_psum, 1)
                if not first:
                    for j in range(CG):
                        if j == 0:
                            pe.wait_ge(yT_done, h)
                        out_chunk(q + 3, j, (j + 1) % 2, (u1 + 1, u0 + 2, u1 + 2, u0 + 3)[j])
                pe.wait_ge(y_ready, h + 1)
                transpose_tiles(y_sb, (2, 3)).then_inc(yT_psum, 1)

            retention(0)
            with pe.Fori(1, H) as h:
                retention(h)
            pe.wait_ge(yT_done, H)
            u0, u1 = RET_TAIL_USES
            for j in range(CG):
                out_chunk(RET_TAIL_Q, j, (j + 1) % 2, (u1, u0, u1 + 1, u0 + 1)[j])
                if j:
                    transpose_norm(1, j - 1)

            for c in range(24):
                i = c // 4
                if c < 4:
                    pe.wait_ge(hT_done, CG + c + 1)
                in_chunk(KV_Q + i, c, (i + 1) % 2, (KV_USES[1] + i // 2, KV_USES[0] + i // 2)[i % 2])
                if c == 0:
                    transpose_norm(1, 3)
                if c in (4, 8, 12, 20):
                    n = (4, 8, 12, 20).index(c)
                    before = c // 4 - 1
                    pe.wait_ge(acc_free[(before + 1) % 2], KV_USES[(before + 1) % 2] + before // 2 + 1)
                    if n == 0:
                        pe.wait_ge(hT_done, 2 * CG)
                    else:
                        pe.wait_ge(rawT_ready, n)
                    transpose_tiles(stage, (0, 1)).then_inc(rawT_psum, 1)
                if c in (5, 9):
                    n = c // 4 - 1
                    pe.wait_ge(window_ready, n + 1)
                    pe.wait_ge(w1_in, 32 + 16 * n)
                    for l in range(CMP_LEN):
                        ins = pe.matmul(side[2][:, 0:G * NC], w1[:, l, :], window[:, l, :], start=(l == 0), stop=(l == CMP_LEN - 1))
                    ins.then_inc(hid_psum, 1)
                if c in (6, 10):
                    n = c // 4 - 1
                    pe.wait_ge(hid_ready, n + 1)
                    pe.wait_ge(w2_in, 16 * n + 16)
                    if n == 0:
                        pe.matmul(side[3][:, 0:G * NC], w2[:, :], hidden[:, :], start=True, stop=True).then_inc(cmp_psum, 1)
                    else:
                        pe.wait_ge(cmp_ready, 1)
                        for g in range(G):
                            ins = pe.matmul(side[3][0:NC, g * DH:(g + 1) * DH], hidden[:, g * NC:(g + 1) * NC], w2[:, :], start=True, stop=True)
                        ins.then_inc(cmp_psum, 1)
                if c == 23:
                    pe.wait_ge(gw_done, 1)
                    pe.wait_ge(acc_free[1], NSA_USES[1] - 1)
                    ghi = yT_hi[:, 0:3, :].rearrange("p a b -> p (a b)")
                    glo = yT_lo[:, 0:3, :].rearrange("p a b -> p (a b)")
                    for t in range(TT):
                        tok = slice(t * P, (t + 1) * P)
                        for k in range(KT):
                            w = slice(k * NG, (k + 1) * NG)
                            o = acc[1][t][:, 0:NG]
                            pe.matmul(o, hT_hi[:, k, tok], ghi[:, w], start=(k == 0), stop=False)
                            pe.matmul(o, hT_hi[:, k, tok], glo[:, w], start=False, stop=False)
                            ins = pe.matmul(o, hT_lo[:, k, tok], ghi[:, w], start=False, stop=(k == KT - 1))
                    ins.then_inc(gates_psum, 1)

            def head_scores(g, r):
                u = R * g + r
                if type(u) is not int or u > 0:
                    pe.wait_ge(score_read, u)
                for b, keysT in enumerate((ksT, kwT)):
                    keys = keysT[:, bass.ds(g, 1), :].rearrange("p a b -> p (a b)")
                    pe.matmul(side[2 + b][:, 0:P], qhT[:, r, 0:P], keys[:, 0:P], start=True, stop=True)
                    ins = pe.matmul(side[2 + b][:, P:3 * P], qhT[:, r, P:2 * P], keys, start=True, stop=True)
                    if b == 0:
                        for t in range(TT):
                            at = 3 * P + t * NC
                            pe.matmul(side[2][:, at:at + NC], qhT[:, r, t * P:(t + 1) * P], kcmpT[:, bass.ds(g * NC, NC)], start=True, stop=True)
                ins.then_inc(score_psum, 1)

            def transpose_probs(g, r):
                u = R * g + r
                pe.wait_ge(prob_ready, u + 1)
                if type(u) is not int or u > 0:
                    pe.wait_ge(pT_ready, u)
                for b in range(2):
                    for i in range(3):
                        pe.transpose(side[b][:, i * P:(i + 1) * P], prob[:, b, i * P:(i + 1) * P], ident[:, :])
                    ins = pe.transpose(side[b][0:NC, 3 * P:4 * P], prob_c[:, b, :], ident[:, :])
                ins.then_inc(pT_psum, 1)

            def weighted_values(g):
                pe.wait_ge(pT_ready, R * g + R)
                pe.wait_ge(v_now_ready, g + 1)
                pe.wait_ge(score_read, R * g + R)
                for t, tiles in enumerate((((0, 0),), ((1, 0), (2, 1)))):
                    first = True
                    for b in range(2):
                        for tile, keys in tiles:
                            pe.matmul(side[2 + t][:, :], v_now[:, 2 * b + keys, :], pT[:, b, tile, :], start=first, stop=False)
                            first = False
                    ins = pe.matmul(side[2 + t][:, :], vc_now[:, :], pTc[0:NC, t, :], start=False, stop=True)
                ins.then_inc(pv_psum, 1)
                pe.wait_ge(acc_free[1], nsa_uses(g)[1] + 1)
                transpose_tiles(stage, (0, 1)).then_inc(zT_psum, 1)

            def sparse(g):
                first = type(g) is int and g == 0
                q = nsa_q(g)
                u0, u1 = nsa_uses(g)
                for c in range(8):
                    in_chunk(q + c // 4, c, c // 4, (u0, u1)[c // 4])
                    if c == 4:
                        pe.wait_ge(acc_free[0], u0 + 1)
                        if first:
                            pe.wait_ge(rawT_ready, 4)
                        else:
                            pe.wait_ge(zT_ready, g)
                        transpose_tiles(stage, (0, 1)).then_inc(qh_psum, 1)
                    if not first:
                        if c == 5:
                            pe.wait_ge(qh_ready, g + 1)
                            pe.wait_ge(y32_done, g)
                            head_scores(g, 0)
                        if c >= 6:
                            transpose_probs(g, c - 6)
                            head_scores(g, c - 5)
                if first:
                    pe.wait_ge(qh_ready, 1)
                    pe.wait_ge(late_in, 64)
                    for r in range(R):
                        head_scores(g, r)
                        transpose_probs(g, r)
                    weighted_values(g)
                else:
                    for j in range(CG):
                        if j == 0:
                            pe.wait_ge(nsa_yT_done, g)
                        out_chunk(q + 2, j, j % 2, (u0 + 1, u1 + 1, u0 + 2, u1 + 2)[j])
                        if j < 2:
                            transpose_probs(g, 2 + j)
                        if j < 1:
                            head_scores(g, 3 + j)
                        if j == 2:
                            weighted_values(g)

            sparse(0)
            with pe.Fori(1, G) as g:
                sparse(g)
            u0, u1 = nsa_uses(G)
            pe.wait_ge(nsa_yT_done, G)
            for j in range(CG):
                out_chunk(NSA_TAIL_Q, j, j % 2, (u0, u1, u0 + 1, u1 + 1)[j])


_INS = ["x", "norm_g", "ret_w_in", "ret_w_out", "nsa_w_in", "nsa_cmp_pos_k", "nsa_cmp_w1_k", "nsa_cmp_w2_k",
        "nsa_cmp_pos_v", "nsa_cmp_w1_v", "nsa_cmp_w2_v", "nsa_w_out", "final_g"]


def shape_constants(S, NC):
    import numpy as np
    p = np.arange(P)
    log_g = np.log1p(-np.exp2(-5.0 - np.arange(RET_HEADS)))
    diff = np.arange(2 * P)[None, :] - p[:, None]
    dk = 2048 // RET_HEADS
    dec = np.where(diff >= 0, np.exp(np.maximum(diff, 0)[None] * log_g[:, None, None]), 0.0) * dk ** -0.5
    slopes = -np.exp2(-8.0 * np.arange(1, NSA_HEADS + 1) / NSA_HEADS)
    far = 1e33

    def masked(d):
        return np.where(d >= 0, d, far)
    tile0 = p[:, None] - p[None, :]
    tile1 = P + p[:, None] - np.arange(2 * P)[None, :]
    ends = np.arange(NC) * CMP_STRIDE + CMP_LEN - 1
    cmp = [t * P + p[:, None] - ends[None, :] for t in range(2)]
    f = np.float32
    return {
        "identity": np.eye(P, dtype=f),
        "decay": np.ascontiguousarray(dec.transpose(1, 0, 2)).astype(f),
        "neg_slopes": np.broadcast_to(slopes, (P, NSA_HEADS)).astype(f),
        "distance": np.concatenate([masked(tile0), masked(tile1)], 1).astype(f),
        "distance_cmp": np.concatenate([masked(c) for c in cmp], 1).astype(f),
        "cmp_seen": (p[:, None] >= CMP_LEN - 1).astype(f),
    }


def kernel(**inputs):
    import numpy as _np
    import concourse.bacc as _bacc
    from concourse import mybir as _mybir
    from concourse.bass_utils import run_bass_kernel_spmd as _run

    nc = _bacc.Bacc("TRN2", target_bir_lowering=False, num_devices=1)
    arrays, args = {}, []
    given = {name: _np.ascontiguousarray(inputs[name]) for name in _INS}
    S = given["x"].shape[1]
    given.update(shape_constants(S, (S - CMP_LEN) // CMP_STRIDE + 1))
    for name, a in given.items():
        arrays[f"in_{name}"] = a
        args.append(nc.dram_tensor(f"in_{name}", a.shape, _mybir.dt.from_np(a.dtype), kind="ExternalInput").ap())
    args.append(nc.dram_tensor("out_0", given["x"].shape, _mybir.dt.float32, kind="ExternalOutput").ap())
    trunk(nc, *args)
    r = _run(nc, [arrays], core_ids=[0])
    return r.results[0]["out_0"]
```

```python
from contextlib import ExitStack

import concourse.bass as bass
from concourse import mybir

F32 = mybir.dt.float32
F32R = mybir.dt.float32r
ACT = mybir.ActivationFunctionType
ALU = mybir.AluOpType
AX = mybir.AxisListType

P = 128
EPS = 1e-6
COLS = 512
KPC = 4
RING = 4
BRANCHES = 3
CMP_LEN, CMP_STRIDE = 32, 16
RET_HEADS = 8
NSA_HEADS = 16


def trunk(nc, x, norm_g, ret_w_in, ret_w_out, nsa_w_in, cmp_pos_k, cmp_w1_k, cmp_w2_k, cmp_pos_v,
          cmp_w1_v, cmp_w2_v, nsa_w_out, final_g, identity, decay, neg_slopes, distance,
          cmp_seen, out):
    _, S, D = x.shape
    TT = S // P
    KT = D // P
    H = RET_HEADS
    DK = D // H
    G = NSA_HEADS // 4
    R = NSA_HEADS // G
    DH = D // NSA_HEADS
    KV = G * DH
    NC = (S - CMP_LEN) // CMP_STRIDE + 1
    NG = NSA_HEADS * BRANCHES
    GATE_COL = D + 6 * KV
    Z_COL = GATE_COL + NG
    CG = D // COLS
    FULL = [(NC, NC + P), (2 * NC + P, 2 * NC + 3 * P)]
    CMP_AT = [0, NC + P]
    SCORES = 2 * NC + 3 * P
    assert TT == 2 and DK == 256 and KV == COLS and R * DH == COLS and CG == RING == KPC == 4

    ret_in = ret_w_in[0].rearrange("(k p) n -> p k n", p=P)
    ret_out = ret_w_out[0].rearrange("(k p) n -> p k n", p=P)
    nsa_in = nsa_w_in[0].rearrange("(k p) n -> p k n", p=P)
    nsa_out = nsa_w_out[0].rearrange("(k p) n -> p k n", p=P)
    x_rows = x[0].rearrange("(t p) d -> p t d", p=P)
    out_rows = out[0].rearrange("(t p) d -> p t d", p=P)

    with ExitStack() as ctx:
        def sb(name, shape, dt=F32):
            return ctx.enter_context(nc.sbuf_tensor(name, shape, dt))

        def sem(name):
            return ctx.enter_context(nc.semaphore(name))

        w_raw = sb("w_raw", [P, RING, KPC, COLS])
        w_hi = sb("w_hi", [P, RING, KPC, COLS], F32R)
        w_lo = sb("w_lo", [P, RING, KPC, COLS], F32R)
        hT_hi = sb("hT_hi", [P, KT, S], F32R)
        hT_lo = sb("hT_lo", [P, KT, S], F32R)
        yT_hi = sb("yT_hi", [P, KPC, S], F32R)
        yT_lo = sb("yT_lo", [P, KPC, S], F32R)
        res = sb("res", [P, TT, D])
        stage = sb("stage", [P, TT, COLS])
        ksT = sb("ksT", [P, G, NC + S])
        kwT = sb("kwT", [P, G, S])
        vs = sb("vs", [P, TT, KV])
        vw = sb("vw", [P, TT, KV])
        ident = sb("ident", [P, P])
        dist = sb("dist", [P, SCORES])
        seen = sb("seen", [P, 1])
        slopes = sb("slopes", [P, NSA_HEADS])
        cols = sb("cols", [P, 96])
        gates = sb("gates", [P, TT, NG])
        vcmp = sb("vcmp", [NC, G * DH])
        sumsq = sb("sumsq", [P, TT, CG])
        meansq = sb("meansq", [P, TT])
        rstd = sb("rstd", [P, 3, TT])
        minus_half = sb("minus_half", [P, TT])
        bn6 = sb("bn6", [P, TT, 6])
        mv = sb("mv", [P, TT, 2])
        eps = sb("eps", [P, TT])
        head_rstd = sb("head_rstd", [P, TT])
        negmax = sb("negmax", [P, TT, BRANCHES])
        sums = sb("sums", [P, TT, BRANCHES])
        factor = sb("factor", [P, TT, BRANCHES])

        last_head_yT = hT_hi[:, KT - KPC:KT, :], hT_lo[:, KT - KPC:KT, :]
        last_group_yT = hT_hi[:, 0:KPC, :], hT_lo[:, 0:KPC, :]

        arena = sb("arena", [P, 7616])

        def piece(at, *dims):
            n = 1
            for d in dims:
                n *= d
            v = arena[:, at:at + n]
            if len(dims) == 2:
                v = v.rearrange("p (a b) -> p a b", a=dims[0])
            if len(dims) == 3:
                v = v.rearrange("p (a b c) -> p a b c", a=dims[0], b=dims[1])
            return v

        decays = piece(0, H, 2 * P)
        v_sb = piece(2048, TT, COLS)
        silu_gate = piece(3072, TT, COLS)
        y_sb = piece(4096, TT, COLS)
        qT = piece(5120, 2, S)
        kT = piece(5632, 2, S)
        sT = piece(6144, 3 * P)
        w1 = piece(0, CMP_LEN, DH)
        rawT = piece(4096, G, S)
        window = piece(5120, CMP_LEN, G * NC)
        vw_row = vw[:, :, :].rearrange("p t n -> p (t n)")
        gate_w = vw_row[:, 0:KT * NG].rearrange("p (k n) -> p k n", k=KT)
        w2 = vw_row[:, KT * NG:KT * NG + DH]
        hidden = vw_row[:, KT * NG + DH:KT * NG + DH + G * NC]
        pT = piece(0, 2, 3, R * P)
        pTc = piece(3072, TT, R * P)
        silu_zT = piece(4096, R, S)
        y32 = silu_zT
        qhT = piece(5120, R, S)
        prob = piece(6144, 2, SCORES)
        v_now = piece(6144 + 2 * SCORES, 4, P)
        gatesT = arena[0:NG, 6144:6144 + S]
        vc_now = arena[0:NC, 7488:7488 + DH]
        final_gain = piece(0, D)
        gained = w_raw[:, :, 0:TT, :]

        pair_banks = [[ctx.enter_context(nc.psum_tensor(f"acc{a}{t}", [P, COLS], F32)) for t in range(TT)] for a in range(2)]
        side = [ctx.enter_context(nc.psum_tensor(f"side{i}", [P, COLS], F32)) for i in range(4)]
        acc = pair_banks + [side[0:2]]

        raw_in = [sem(f"raw_in{s}") for s in range(RING)]
        hi_done, lo_done = sem("hi_done"), sem("lo_done")
        chunk_done = sem("chunk_done")
        acc_free = [sem("acc_free0"), sem("acc_free1")]
        x_in = [sem(f"x_in{j}") for j in range(CG)]
        const_in, cols_in, pos_in, late_in = sem("const_in"), sem("cols_in"), sem("pos_in"), sem("late_in")
        w1_in, w2_in, gain_in = sem("w1_in"), sem("w2_in"), sem("gain_in")
        stored = sem("stored")
        cols_psum, cols_ready = sem("cols_psum"), sem("cols_ready")
        hT_psum, hT_hi_done, hT_done = sem("hT_psum"), sem("hT_hi_done"), sem("hT_done")
        squares_done, meansq_done, rstd_step, rstd_done = sem("squares_done"), sem("meansq_done"), sem("rstd_step"), sem("rstd_done")
        const_made, table_loaded = sem("const_made"), sem("table_loaded")
        qkT_psum, qT_ready, kT_ready = sem("qkT_psum"), sem("qT_ready"), sem("kT_ready")
        sT_psum, sT_ready, o_psum = sem("sT_psum"), sem("sT_ready"), sem("o_psum")
        stats_done, mv_done, head_rstd_step, head_rstd_done = sem("stats_done"), sem("mv_done"), sem("head_rstd_step"), sem("head_rstd_done")
        side_read = sem("side_read")
        y_ready = sem("y_ready")
        yT_psum, yT_hi_done, yT_done = sem("yT_psum"), sem("yT_hi_done"), sem("yT_done")
        rawT_psum, rawT_ready = sem("rawT_psum"), sem("rawT_ready")
        window_ready, hid_psum, hid_ready, cmp_psum, cmp_ready = sem("window_ready"), sem("hid_psum"), sem("hid_ready"), sem("cmp_psum"), sem("cmp_ready")
        gw_hi, gw_done, gates_psum, gates_ready = sem("gw_hi"), sem("gw_done"), sem("gates_psum"), sem("gates_ready")
        gatesT_psum, gatesT_ready = sem("gatesT_psum"), sem("gatesT_ready")
        qh_psum, qh_ready = sem("qh_psum"), sem("qh_ready")
        score_psum, score_read, negmax_ready, exp_done = sem("score_psum"), sem("score_read"), sem("negmax_ready"), sem("exp_done")
        recip_done, factor_done, prob_ready = sem("recip_done"), sem("factor_done"), sem("prob_ready")
        pT_psum, pT_ready, v_now_ready, pv_psum = sem("pT_psum"), sem("pT_ready"), sem("v_now_ready"), sem("pv_psum")
        zT_psum, zT_ready = sem("zT_psum"), sem("zT_ready")
        y32_done, nsa_hi_done, nsa_yT_done = sem("y32_done"), sem("nsa_hi_done"), sem("nsa_yT_done")
        gained_done, final_dve, final_act = sem("gained_done"), sem("final_dve"), sem("final_act")

        RET_C = 16
        RET_OUT_PAIR = (1, 0, 1, 2)

        def ret_q(h):
            return 4 * h - 1 if not (type(h) is int and h == 0) else 0
        RET_TAIL_Q = 4 * H - 1
        KV_Q = RET_TAIL_Q + 1
        KV_COLS = [D + i * KV for i in range(5)] + [0, D + 5 * KV]
        KV_GROUPS = len(KV_COLS)

        def nsa_q(g):
            return KV_Q + KV_GROUPS + 3 * g - (0 if type(g) is int and g == 0 else 1)
        NSA_TAIL_Q = nsa_q(G - 1) + 2

        def nsa_chunks(g):
            return ["z"] * 4 + ([] if type(g) is int and g == G - 1 else ["q"] * 4) + ([] if type(g) is int and g == 0 else ["out"] * 4)

        def ret_uses(h):
            return (3 * h - 1, 3 * h - 2) if not (type(h) is int and h == 0) else (0, 0)
        RET_TAIL_USES = (3 * H - 1, 3 * H - 2)

        def side_reads(h):
            return 2 * h - 1
        KV_USES = (RET_TAIL_USES[0] + 2, RET_TAIL_USES[1] + 2)
        NSA_USES = (KV_USES[0] + 4, KV_USES[1] + 4)

        def nsa_uses(g):
            first = type(g) is int and g == 0
            return tuple(u if first else u + 3 * g - 2 for u in NSA_USES)
        SLOTS = {12: dict(scores=(0, 2, 4, 6), factors=(1, 3, 5, 7), probsT=(2, 4, 6, 8), zT=5, values=9, qT=9, sum=10),
                 8: dict(scores=(0, 2, 4, 6), factors=(1, 3, 5, 7), probsT=(2, 4, 6, 7), zT=5, values=7, qT=7, sum=7)}
        NSA_TAIL_USES = (nsa_uses(G - 1)[0] + 2, nsa_uses(G - 1)[1] + 3)

        def out_pair(g, j):
            return j % 2 if type(g) is int and g == G - 1 else (j + 1) % 2

        def out_projected(g):
            return chunk_done, 4 * nsa_q(g) + len(nsa_chunks(g))

        def group_yT(g):
            return last_group_yT if type(g) is int and g == G - 1 else (yT_hi, yT_lo)

        def added(n, j):
            pair = (j + n) % 2
            return acc_free[pair], (RET_TAIL_USES if n == 1 else NSA_TAIL_USES)[pair] + j // 2 + 1

        block = ctx.enter_context(nc.Block())

        @block.sync
        def _(sp):
            def chunk(q, s, halves):
                if not (type(q) is int and q == 0):
                    sp.wait_ge(lo_done, 4 * q + s - 3)
                for to, src in halves:
                    sp.dma_start(to, src).then_inc(raw_in[s], 16)

            def by_rows(s, w, k0, col):
                return [(w_raw[:, s, 2 * i:2 * i + 2, :], w[:, bass.ds(k0 + 2 * i, 2), bass.ds(col, COLS)]) for i in range(2)]

            def by_columns(s, w, k0, col_a, col_b):
                return [(w_raw[:, s, :, i * DK:(i + 1) * DK], w[:, k0:k0 + KPC, bass.ds(c, DK)]) for i, c in enumerate((col_a, col_b))]

            def ret_inputs(h):
                q = ret_q(h)
                for c in range(12):
                    s = c % RING
                    if c < 4:
                        if type(h) is int and h == 0:
                            sp.dma_start(res[:, :, s * COLS:(s + 1) * COLS], x_rows[:, :, s * COLS:(s + 1) * COLS]).then_inc(x_in[s], 16)
                        chunk(q, s, by_columns(s, ret_in, KPC * s, h * DK, D + h * DK))
                    elif c < 8:
                        chunk(q + 1, s, by_rows(s, ret_in, KPC * s, 2 * D + h * COLS))
                    else:
                        chunk(q + 2, s, by_rows(s, ret_in, KPC * s, 4 * D + h * COLS))

            def outputs(q, w, head):
                for j in range(CG):
                    chunk(q, j, by_rows(j, w, head * KPC, j * COLS))

            ret_inputs(0)
            with sp.Fori(1, H) as h:
                ret_inputs(h)
                outputs(ret_q(h) + 3, ret_out, h - 1)
            outputs(RET_TAIL_Q, ret_out, H - 1)
            for i, col in enumerate(KV_COLS):
                for s in range(RING):
                    chunk(KV_Q + i, s, by_rows(s, nsa_in, KPC * s, col))

            def sparse(g):
                for c, kind in enumerate(nsa_chunks(g)):
                    at, s = nsa_q(g) + c // RING, c % RING
                    if kind == "z":
                        chunk(at, s, by_rows(s, nsa_in, KPC * s, Z_COL + g * COLS))
                    elif kind == "q":
                        chunk(at, s, by_rows(s, nsa_in, KPC * s, g * COLS + COLS))
                    else:
                        chunk(at, s, by_rows(s, nsa_out, (g - 1) * KPC, s * COLS))

            sparse(0)
            with sp.Fori(1, G - 1) as g:
                sparse(g)
            sparse(G - 1)
            outputs(NSA_TAIL_Q, nsa_out, G - 1)
            for i in range(2):
                for t in range(TT):
                    sp.wait_ge((final_dve, final_act)[t], i + 1)
                    sp.dma_start(out_rows[:, t, :].rearrange("p (j n) -> p j n", j=CG)[:, 2 * i:2 * i + 2, :],
                                 gained[:, 2 * i:2 * i + 2, t, :]).then_inc(stored, 16)
            sp.wait_ge(stored, 16 * 2 * TT)

        @block.gpsimd
        def _(pool):
            pool.dma_start(stage[2 * KT:2 * KT + CMP_LEN, 0, 0:P], cmp_pos_k[0]).then_inc(pos_in, 16)
            pool.dma_start(stage[2 * KT + CMP_LEN:96, 0, 0:P], cmp_pos_v[0]).then_inc(pos_in, 16)
            pool.memset(minus_half[:, :], -0.5).then_inc(const_made, 1)
            pool.wait_ge(x_in[CG - 1], 16)
            pool.dma_start(decays, decay).then_inc(const_in, 16)
            pool.dma_start(slopes[:, :], neg_slopes).then_inc(late_in, 16)
            pool.dma_start(dist[:, :], distance).then_inc(late_in, 16)
            pool.dma_start(seen[:, :], cmp_seen).then_inc(late_in, 16)
            pool.wait_ge(const_made, 1)

            def token_factor(n):
                pool.wait_ge(meansq_done, n + 1)
                pool.tensor_scalar(meansq[:, :], meansq[:, :], 1.0 / D, EPS, ALU.mult, ALU.add).then_inc(rstd_step, 1)
                pool.wait_ge(rstd_step, n + 1)
                pool.tensor_tensor(rstd[:, n, :], meansq[:, :], minus_half[:, :], ALU.pow).then_inc(rstd_done, 1)

            def head_factor(h):
                pool.wait_ge(mv_done, TT * h + TT)
                pool.tensor_tensor(head_rstd[:, :], mv[:, :, 1], eps[:, :], ALU.add).then_inc(head_rstd_step, 1)
                pool.wait_ge(head_rstd_step, h + 1)
                pool.tensor_tensor(head_rstd[:, :], head_rstd[:, :], minus_half[:, :], ALU.pow).then_inc(head_rstd_done, 1)

            token_factor(0)
            head_factor(0)
            with pool.Fori(1, H) as h:
                head_factor(h)
            pool.wait_ge(yT_done, H)
            pool.dma_start(w1, cmp_w1_k[0].rearrange("(l d) n -> d l n", d=DH)).then_inc(w1_in, 16)
            pool.dma_start(w2[:, :], cmp_w2_k[0]).then_inc(w2_in, 16)
            pool.dma_start(gate_w, nsa_in[:, :, GATE_COL:GATE_COL + NG]).then_inc(w1_in, 16)
            token_factor(1)
            pool.wait_ge(hid_psum, 1)
            pool.dma_start(w1, cmp_w1_v[0].rearrange("(l d) n -> d l n", d=DH)).then_inc(w1_in, 16)
            pool.wait_ge(cmp_psum, 1)
            pool.dma_start(w2[:, :], cmp_w2_v[0]).then_inc(w2_in, 16)

            def group_values(g):
                if not (type(g) is int and g == 0):
                    pool.wait_ge(pv_psum, g)
                for b, v in enumerate((vs, vw)):
                    pool.tensor_copy(v_now[:, 2 * b:2 * b + 2, :], v[:, :, bass.ds(g * DH, DH)])
                pool.tensor_copy(vc_now[:, :], vcmp[:, bass.ds(g * DH, DH)]).then_inc(v_now_ready, 1)

            pool.wait_ge(gates_ready, 1)
            pool.wait_ge(cmp_ready, 2)
            group_values(0)
            with pool.Fori(1, G) as g:
                group_values(g)
            pool.wait_ge(pv_psum, G)
            pool.dma_start(final_gain, final_g.rearrange("(o d) -> o d", o=1).to_broadcast([P, D])).then_inc(gain_in, 16)
            token_factor(2)

        @block.scalar
        def _(act):
            def high(q, s):
                act.wait_ge(raw_in[s], 32 * q + 32)
                if not (type(q) is int and q == 0):
                    act.wait_ge(chunk_done, 4 * q + s - 3)
                act.copy(w_hi[:, s, :, :], w_raw[:, s, :, :]).then_inc(hi_done, 1)

            def ahead(q, c):
                high(q + (c + 2) // RING, (c + 2) % RING)

            def norm_high(layer, j):
                act.wait_ge(hT_psum, CG * layer + j + 1)
                if layer == 0 and j == 0:
                    act.wait_ge(cols_ready, 1)
                for i in range(KPC):
                    k = KPC * j + i
                    ins = act.activation(hT_hi[:, k, :], side[2 * (j % 2) + i // 2][:, (i % 2) * S:(i % 2 + 1) * S], ACT.Copy,
                                         scale=cols[:, KT * layer + k:KT * layer + k + 1])
                ins.then_inc(hT_hi_done, 1)

            def squares(n, j):
                if n == 0:
                    act.wait_ge(x_in[j], 16)
                    act.wait_ge(cols_psum, 1)
                else:
                    act.wait_ge(*added(n, j))
                if n or j:
                    act.wait_ge(squares_done, CG * n + j)
                for t in range(TT):
                    ins = act.activation(stage[:, t, :], res[:, t, j * COLS:(j + 1) * COLS], ACT.Square, accum_out=sumsq[:, t, j:j + 1])
                ins.then_inc(squares_done, 1)

            act.dma_start(ident[:, :], identity).then_inc(cols_in, 16)
            act.dma_start(stage[0:2 * KT, 0, 0:P], norm_g.rearrange("l (k p) -> (l k) p", p=P)).then_inc(cols_in, 16)
            act.wait_ge(const_made, 1)
            act.activation(eps[:, :], minus_half[:, :], ACT.Square).then_inc(table_loaded, 1)
            norm_high(0, 0)
            high(0, 0)
            norm_high(0, 1)
            high(0, 1)
            squares(0, 0)
            squares(0, 1)

            def high_yT(h):
                act.wait_ge(yT_psum, h + 1)
                to = last_head_yT[0] if type(h) is int and h == H - 1 else yT_hi
                for i in range(2):
                    act.copy(to[:, 2 * i:2 * i + 2, :], side[2 + i][:, :].rearrange("p (a b) -> p a b", a=2)).then_inc(yT_hi_done, 1)

            def retention(h):
                first = type(h) is int and h == 0
                q = ret_q(h)
                n0 = 4 * q
                for c in range(12 if first else RET_C):
                    ahead(q, c)
                    if first and c < 2:
                        norm_high(0, 2 + c)
                    if first and c < 2:
                        squares(0, 2 + c)
                    if c == 4:
                        act.wait_ge(qkT_psum, h + 1)
                        act.copy(qT, side[0][:, :].rearrange("p (a b) -> p a b", a=2)).then_inc(qT_ready, 1)
                    if c == 7:
                        act.wait_ge(chunk_done, n0 + 8)
                        for t in range(TT):
                            ins = act.activation(v_sb[:, t, :], acc[1][t][:, :], ACT.Copy, scale=rstd[:, 0, t:t + 1])
                        ins.then_inc(acc_free[1], 1)
                    if c == 11:
                        act.wait_ge(chunk_done, n0 + 12)
                        for t in range(TT):
                            ins = act.activation(silu_gate[:, t, :], acc[0][t][:, :], ACT.Silu, scale=rstd[:, 0, t:t + 1])
                        ins.then_inc(acc_free[0], 1)
                    if c == (11 if first else 12):
                        act.wait_ge(side_read, 1 if first else side_reads(h) + 1)
                        act.wait_ge(head_rstd_done, h + 1)
                        for t in range(TT):
                            ins = act.activation(y_sb[:, t, :], y_sb[:, t, :], ACT.Copy, scale=head_rstd[:, t:t + 1])
                        ins.then_inc(y_ready, 1)
                    if c == 0 and not first:
                        high_yT(h - 1)
                    if c == 14 and type(h) is int:
                        high_yT(h)

            retention(0)
            with act.Fori(1, H - 1) as h:
                retention(h)
            retention(H - 1)
            for j in range(CG):
                ahead(RET_TAIL_Q, j)
                if j:
                    norm_high(1, j - 1)
                squares(1, j)

            def take_q(g):
                act.wait_ge(qh_psum, g + 1)
                for i in range(2):
                    ins = act.activation(qhT[:, 2 * i:2 * i + 2, :], side[i][:, :].rearrange("p (a b) -> p a b", a=2), ACT.Copy, scale=float(DH) ** -0.5)
                ins.then_inc(qh_ready, 1)

            def compress(i, bank):
                act.wait_ge(hid_psum, i + 1)
                act.activation(hidden[:, :], side[bank][:, 0:G * NC], ACT.Silu).then_inc(hid_ready, 1)

            for c in range(4 * KV_GROUPS):
                ahead(KV_Q, c)
                if c == 0:
                    norm_high(1, 3)
                if c == 24:
                    take_q(0)
                if c in (4, 8, 12, 20):
                    n = (4, 8, 12, 20).index(c)
                    to = (rawT, rawT, ksT[:, :, NC:NC + S], kwT[:, :, :])[n]
                    act.wait_ge(rawT_psum, n + 1)
                    if n == 1:
                        act.wait_ge(window_ready, 1)
                    for i in range(2):
                        ins = act.copy(to[:, 2 * i:2 * i + 2, :], side[i][:, :].rearrange("p (a b) -> p a b", a=2))
                    ins.then_inc(rawT_ready, 1)
                if c in (5, 9):
                    compress(0 if c == 5 else 1, 2)
                if c in (6, 10):
                    n = 0 if c == 6 else 1
                    act.wait_ge(cmp_psum, n + 1)
                    if n == 0:
                        act.copy(ksT[:, :, 0:NC], side[3][:, 0:G * NC].rearrange("p (g c) -> p g c", g=G)).then_inc(cmp_ready, 1)
                    else:
                        act.copy(vcmp[:, :], side[3][0:NC, :]).then_inc(cmp_ready, 1)
                if c == 16:
                    act.wait_ge(w1_in, 32)
                    act.copy(yT_hi[:, 0:3, :].rearrange("p a b -> p (a b)"), gate_w.rearrange("p a b -> p (a b)")).then_inc(gw_hi, 1)
                if c == 27:
                    act.wait_ge(gates_psum, 1)
                    for t in range(TT):
                        ins = act.activation(gates[:, t, :], acc[0][1][:, t * NG:(t + 1) * NG], ACT.Sigmoid, scale=rstd[:, 1, t:t + 1])
                    ins.then_inc(acc_free[0], 1)

            def head_exps(g, r):
                u = R * g + r
                act.wait_ge(negmax_ready, u + 1)
                for b in range(2):
                    for t, (a, z) in enumerate(FULL):
                        act.activation(prob[:, b, a:z], prob[:, b, a:z], ACT.Exp, bias=negmax[:, t, b + 1:b + 2],
                                       accum_out=sums[:, t, b + 1:b + 2])
                for t, a in enumerate(CMP_AT):
                    ins = act.activation(prob[:, 0, a:a + NC], prob[:, 0, a:a + NC], ACT.Exp, bias=negmax[:, t, 0:1], accum_out=sums[:, t, 0:1])
                ins.then_inc(exp_done, 1)

            def take_pT(g, r):
                act.wait_ge(pT_psum, R * g + r + 1)
                for b in range(2):
                    act.copy(pT[:, b, :, r * P:(r + 1) * P], side[b][:, 0:3 * P].rearrange("p (a b) -> p a b", a=3))
                    ins = act.copy(pTc[0:NC, b, r * P:(r + 1) * P], side[b][0:NC, 3 * P:4 * P])
                ins.then_inc(pT_ready, 1)

            def take_z(q):
                act.wait_ge(chunk_done, 4 * q + 4)
                for t in range(TT):
                    ins = act.activation(stage[:, t, :], acc[1][t][:, :], ACT.Silu, scale=rstd[:, 1, t:t + 1])
                ins.then_inc(acc_free[1], 1)

            def take_zT(g):
                act.wait_ge(zT_psum, g + 1)
                for i in range(2):
                    ins = act.copy(silu_zT[:, 2 * i:2 * i + 2, :], side[i][:, :].rearrange("p (a b) -> p a b", a=2))
                ins.then_inc(zT_ready, 1)

            def high_y(g):
                if type(g) is not int or g in range(1, G - 1):
                    act.wait_ge(*out_projected(g))
                for t in range(TT):
                    tok = slice(t * P, (t + 1) * P)
                    act.wait_ge(y32_done, TT * g + t + 1)
                    act.copy(group_yT(g)[0][:, :, tok], y32[:, :, tok]).then_inc(nsa_hi_done, 1)

            def sparse(g):
                q = nsa_q(g)
                kinds = nsa_chunks(g)
                at = SLOTS[len(kinds)]
                for c, kind in enumerate(kinds):
                    ahead(q, c)
                    if c == 3:
                        take_z(q)
                    if c in at["probsT"]:
                        take_pT(g, at["probsT"].index(c))
                    if c in at["scores"]:
                        head_exps(g, at["scores"].index(c))
                    if c == at["zT"]:
                        take_zT(g)
                    if c == at["qT"] and "q" in kinds:
                        take_q(g + 1)
                high_y(g)

            sparse(0)
            with act.Fori(1, G - 1) as g:
                sparse(g)
            sparse(G - 1)
            for j in range(CG):
                if j < 2:
                    ahead(NSA_TAIL_Q, j)
                squares(2, j)
            act.wait_ge(rstd_done, 3)
            act.wait_ge(gained_done, CG)
            for i in range(2):
                at = gained[:, 2 * i:2 * i + 2, 1, :]
                act.activation(at, at, ACT.Copy, scale=rstd[:, 2, 1:2]).then_inc(final_act, 1)

        @block.vector
        def _(dve):
            def low(q, s):
                dve.wait_ge(hi_done, 4 * q + s + 1)
                dve.tensor_tensor(w_lo[:, s, :, :], w_raw[:, s, :, :], w_hi[:, s, :, :].bitcast(F32), ALU.subtract).then_inc(lo_done, 1)

            def ahead(q, c):
                low(q + (c + 2) // RING, (c + 2) % RING)

            def norm_low(layer, j):
                dve.wait_ge(hT_hi_done, CG * layer + j + 1)
                for i in range(KPC):
                    k = KPC * j + i
                    ins = dve.scalar_tensor_tensor(out=hT_lo[:, k, :], in0=side[2 * (j % 2) + i // 2][:, (i % 2) * S:(i % 2 + 1) * S],
                                                   scalar=cols[:, KT * layer + k:KT * layer + k + 1], in1=hT_hi[:, k, :].bitcast(F32),
                                                   op0=ALU.mult, op1=ALU.subtract)
                ins.then_inc(hT_done, 1)

            def mean_square(n):
                dve.wait_ge(squares_done, CG * n + CG)
                if n:
                    dve.wait_ge(rstd_done, n)
                dve.tensor_reduce(meansq[:, :], sumsq[:, :, :], AX.X, ALU.add).then_inc(meansq_done, 1)

            def add_residual(chunk, pair, j):
                dve.wait_ge(chunk_done, chunk + 1)
                for t in range(TT):
                    at = res[:, t, j * COLS:(j + 1) * COLS]
                    ins = dve.tensor_tensor(at, acc[pair][t][:, :], at, ALU.add)
                ins.then_inc(acc_free[pair] if pair < 2 else side_read, 1)

            def take(chunk, pair, to, layer):
                dve.wait_ge(chunk_done, chunk)
                dve.wait_ge(rstd_done, layer + 1)
                for t in range(TT):
                    ins = dve.tensor_scalar(to[:, t, :], acc[pair][t][:, :], rstd[:, layer, t:t + 1], None, ALU.mult)
                ins.then_inc(acc_free[pair], 1)

            dve.wait_ge(cols_psum, 1)
            dve.tensor_copy(cols[:, :], acc[1][0][:, 0:96]).then_inc(cols_ready, 1)
            dve.wait_ge(cols_ready, 1)
            norm_low(0, 0)
            low(0, 0)
            norm_low(0, 1)
            low(0, 1)

            def head_stats(h):
                dve.wait_ge(o_psum, h + 1)
                for t in range(TT):
                    dve.bn_stats(bn6[:, t, :], side[t][:, :]).then_inc(stats_done, 1)
                dve.wait_ge(stats_done, TT * h + TT)
                if type(h) is int and h == 0:
                    dve.wait_ge(table_loaded, 1)
                dve.memset(eps[:, :], EPS)
                for t in range(TT):
                    dve.bn_aggr(mv[:, t, :], bn6[:, t, :]).then_inc(mv_done, 1)

            def head_y(h):
                dve.wait_ge(acc_free[0], ret_uses(h)[0] + 2)
                dve.wait_ge(mv_done, TT * h + TT)
                for t in range(TT):
                    ins = dve.scalar_tensor_tensor(out=y_sb[:, t, :], in0=side[t][:, :], scalar=mv[:, t, 0:1], in1=silu_gate[:, t, :],
                                                   op0=ALU.subtract, op1=ALU.mult)
                ins.then_inc(side_read, 1)

            def low_yT(h):
                hi, lo = last_head_yT if type(h) is int and h == H - 1 else (yT_hi, yT_lo)
                for i in range(2):
                    dve.wait_ge(yT_hi_done, 2 * h + i + 1)
                    ins = dve.tensor_tensor(lo[:, 2 * i:2 * i + 2, :], side[2 + i][:, :].rearrange("p (a b) -> p a b", a=2),
                                            hi[:, 2 * i:2 * i + 2, :].bitcast(F32), ALU.subtract)
                ins.then_inc(yT_done, 1)

            def retention(h):
                first = type(h) is int and h == 0
                q = ret_q(h)
                for c in range(12 if first else RET_C):
                    ahead(q, c)
                    if first and c < 2:
                        norm_low(0, 2 + c)
                    if first and c == 1:
                        mean_square(0)
                    if c == 3:
                        take(4 * q + 4, 0, stage, 0)
                    if c == 4:
                        dve.wait_ge(qkT_psum, h + 1)
                        dve.tensor_copy(kT, side[1][:, :].rearrange("p (a b) -> p a b", a=2)).then_inc(kT_ready, 1)
                    if c == 5:
                        dve.wait_ge(sT_psum, h + 1)
                        if first:
                            dve.wait_ge(const_in, 16)
                        mask = decays[:, bass.ds(h, 1), :].rearrange("p a b -> p (a b)")
                        dve.tensor_tensor(sT[:, 0:2 * P], side[2][:, 0:2 * P], mask, ALU.mult)
                        dve.tensor_tensor(sT[:, 2 * P:3 * P], side[2][:, 2 * P:3 * P], mask[:, 0:P], ALU.mult).then_inc(sT_ready, 1)
                    if c == 8:
                        head_stats(h)
                    if c >= 12:
                        add_residual(4 * q + c, RET_OUT_PAIR[c - 12], c - 12)
                    if c == (11 if first else 12):
                        head_y(h)
                    if c == 0 and not first:
                        low_yT(h - 1)
                    if c == 14 and type(h) is int:
                        low_yT(h)

            retention(0)
            with dve.Fori(1, H - 1) as h:
                retention(h)
            retention(H - 1)
            for j in range(CG):
                ahead(RET_TAIL_Q, j)
                add_residual(4 * RET_TAIL_Q + j, (j + 1) % 2, j)
                if j:
                    norm_low(1, j - 1)

            def make_window(n):
                dve.wait_ge(rawT_ready, n + 1)
                if n:
                    dve.wait_ge(hid_psum, n)
                pos = cols[:, 2 * KT + CMP_LEN * n:2 * KT + CMP_LEN * (n + 1)]
                for g in range(G):
                    base = rawT[:, g, 0:CMP_LEN]
                    raw_at = bass.AP(base.tensor, base.offset, [base.ap[0], [1, CMP_LEN], [CMP_STRIDE, NC]])
                    pos_at = bass.AP(pos.tensor, pos.offset, [pos.ap[0], [1, CMP_LEN], [0, NC]])
                    ins = dve.tensor_tensor(window[:, :, g * NC:(g + 1) * NC], raw_at, pos_at, ALU.add)
                ins.then_inc(window_ready, 1)

            for c in range(4 * KV_GROUPS):
                ahead(KV_Q, c)
                if c == 0:
                    norm_low(1, 3)
                if c == 1:
                    mean_square(1)
                n = 4 * KV_Q + c + 1
                if c in (3, 7, 11, 19):
                    take(n, (c // 4 + 1) % 2, stage, 1)
                if c in (4, 8):
                    make_window(c // 4 - 1)
                if c == 15:
                    take(n, 0, vs, 1)
                if c == 23:
                    take(n, 0, stage, 1)
                if c == 17:
                    dve.wait_ge(gw_hi, 1)
                    dve.tensor_tensor(yT_lo[:, 0:3, :].rearrange("p a b -> p (a b)"), gate_w.rearrange("p a b -> p (a b)"),
                                      yT_hi[:, 0:3, :].rearrange("p a b -> p (a b)").bitcast(F32), ALU.subtract).then_inc(gw_done, 1)
                if c == 26:
                    dve.wait_ge(gatesT_psum, 1)
                    dve.tensor_copy(gatesT, acc[0][0][0:NG, 0:S]).then_inc(gatesT_ready, 1)
                if c == 27:
                    take(n, 1, vw, 1)
                    dve.wait_ge(acc_free[0], NSA_USES[0])
                    dve.wait_ge(late_in, 48)
                    cmp_gates = gates[:, 0, 0:NG:BRANCHES]
                    dve.tensor_scalar(cmp_gates, cmp_gates, seen[:, 0:1], None, ALU.mult).then_inc(gates_ready, 1)

            def head_scores(g, r):
                u = R * g + r
                dve.wait_ge(score_psum, u + 1)
                slope = slopes[:, bass.ds(g * R + r, 1)]
                dve.scalar_tensor_tensor(out=prob[:, 0, :], in0=dist[:, :], scalar=slope, in1=side[2][:, 0:SCORES], op0=ALU.mult, op1=ALU.add)
                for a, z in FULL:
                    ins = dve.scalar_tensor_tensor(out=prob[:, 1, a:z], in0=dist[:, a:z], scalar=slope, in1=side[3][:, a:z], op0=ALU.mult, op1=ALU.add)
                ins.then_inc(score_read, 1)
                dve.wait_ge(score_read, u + 1)
                for t, (a, z) in enumerate(FULL):
                    dve.tensor_reduce(negmax[:, t, 1:3], prob[:, :, a:z], AX.X, ALU.max, negate=True)
                for t, a in enumerate(CMP_AT):
                    ins = dve.tensor_reduce(negmax[:, t, 0:1], prob[:, 0, a:a + NC], AX.X, ALU.max, negate=True)
                ins.then_inc(negmax_ready, 1)

            def head_probs(g, r):
                u = R * g + r
                dve.wait_ge(exp_done, u + 1)
                dve.reciprocal(sums[:, :, :], sums[:, :, :]).then_inc(recip_done, 1)
                dve.wait_ge(recip_done, u + 1)
                dve.tensor_tensor(factor[:, :, :], sums[:, :, :], gates[:, :, bass.ds(g * R * BRANCHES + r * BRANCHES, BRANCHES)], ALU.mult).then_inc(factor_done, 1)
                dve.wait_ge(factor_done, u + 1)
                for b in range(2):
                    for t, (a, z) in enumerate(FULL):
                        dve.tensor_scalar(prob[:, b, a:z], prob[:, b, a:z], factor[:, t, b + 1:b + 2], None, ALU.mult)
                for t, a in enumerate(CMP_AT):
                    ins = dve.tensor_scalar(prob[:, 0, a:a + NC], prob[:, 0, a:a + NC], factor[:, t, 0:1], None, ALU.mult)
                ins.then_inc(prob_ready, 1)

            def combine(g):
                dve.wait_ge(zT_ready, g + 1)
                dve.wait_ge(pv_psum, g + 1)
                for t in range(TT):
                    dve.tensor_tensor(y32[:, :, t * P:(t + 1) * P], side[2 + t][:, :].rearrange("p (a b) -> p a b", a=R),
                                      silu_zT[:, :, t * P:(t + 1) * P], ALU.mult).then_inc(y32_done, 1)

            def low_y(g):
                hi, lo = group_yT(g)
                for t in range(TT):
                    tok = slice(t * P, (t + 1) * P)
                    dve.wait_ge(nsa_hi_done, TT * g + t + 1)
                    dve.tensor_tensor(lo[:, :, tok], y32[:, :, tok], hi[:, :, tok].bitcast(F32), ALU.subtract).then_inc(nsa_yT_done, 1)

            def sparse(g):
                q = nsa_q(g)
                kinds = nsa_chunks(g)
                at = SLOTS[len(kinds)]
                for c, kind in enumerate(kinds):
                    if c in at["factors"]:
                        head_probs(g, at["factors"].index(c))
                    ahead(q, c)
                    if kind == "out":
                        add_residual(4 * q + c, out_pair(g, c % 4), c % 4)
                    if c == 7 and "q" in kinds:
                        take(4 * q + 8, 0, stage, 1)
                    if c in at["scores"]:
                        head_scores(g, at["scores"].index(c))
                    if c == at["sum"]:
                        combine(g)
                low_y(g)

            sparse(0)
            with dve.Fori(1, G - 1) as g:
                sparse(g)
            sparse(G - 1)
            dve.wait_ge(gain_in, 16)
            for j in range(CG):
                if j < 2:
                    ahead(NSA_TAIL_Q, j)
                add_residual(4 * NSA_TAIL_Q + j, j % 2, j)
                dve.wait_ge(*added(2, j))
                dve.wait_ge(lo_done, 4 * NSA_TAIL_Q + j + 1)
                for t in range(TT):
                    ins = dve.tensor_tensor(gained[:, j, t, :], res[:, t, j * COLS:(j + 1) * COLS], final_gain[:, j * COLS:(j + 1) * COLS], ALU.mult)
                ins.then_inc(gained_done, 1)
            mean_square(2)
            dve.wait_ge(rstd_done, 3)
            dve.wait_ge(gained_done, CG)
            for i in range(2):
                at = gained[:, 2 * i:2 * i + 2, 0, :]
                dve.tensor_scalar(at, at, rstd[:, 2, 0:1], None, ALU.mult).then_inc(final_dve, 1)

        @block.tensor
        def _(pe):
            def chunk(q, s, xT_hi, xT_lo, k0, pair, start, stop, tile_ready=None):
                n = 4 * q + s
                pe.wait_ge(lo_done, n + 1)
                for t in range(TT):
                    if tile_ready:
                        pe.wait_ge(tile_ready[0], tile_ready[1] + t)
                    tok = slice(t * P, (t + 1) * P)
                    for i in range(KPC):
                        a, z = start and i == 0, stop and i == KPC - 1
                        o = acc[pair][t][:, :]
                        pe.matmul(o, xT_hi[:, k0 + i, tok], w_hi[:, s, i, :], start=a, stop=False)
                        pe.matmul(o, xT_hi[:, k0 + i, tok], w_lo[:, s, i, :], start=False, stop=False)
                        ins = pe.matmul(o, xT_lo[:, k0 + i, tok], w_hi[:, s, i, :], start=False, stop=z)
                ins.then_inc(chunk_done, 1)

            def in_chunk(q, c, pair, uses):
                s = c % RING
                if s == 0 and not (type(uses) is int and uses == 0):
                    pe.wait_ge(acc_free[pair], uses)
                chunk(q, s, hT_hi, hT_lo, KPC * s, pair, s == 0, s == RING - 1)

            def out_chunk(q, j, pair, free, uses, hi=yT_hi, lo=yT_lo, tile_ready=None):
                pe.wait_ge(free, uses)
                chunk(q, j, hi, lo, 0, pair, True, True, tile_ready)

            def transpose_norm(layer, j):
                if layer == 0:
                    pe.wait_ge(x_in[j], 16)
                else:
                    pe.wait_ge(*added(1, j))
                if j >= 2:
                    pe.wait_ge(hT_done, CG * layer + j - 1)
                for i in range(KPC):
                    k = KPC * j + i
                    for t in range(TT):
                        at = (i % 2) * S + t * P
                        ins = pe.transpose(side[2 * (j % 2) + i // 2][:, at:at + P], res[:, t, k * P:(k + 1) * P], ident[:, :])
                ins.then_inc(hT_psum, 1)

            def transpose_tiles(src, banks):
                for i in range(4):
                    for t in range(TT):
                        at = (i % 2) * S + t * P
                        ins = pe.transpose(side[banks[i // 2]][:, at:at + P], src[:, t, i * P:(i + 1) * P], ident[:, :])
                return ins

            pe.wait_ge(cols_in, 32)
            transpose_norm(0, 0)
            pe.wait_ge(pos_in, 32)
            pe.transpose(acc[1][0][:, 0:96], stage[0:96, 0, 0:P], ident[0:96, 0:96]).then_inc(cols_psum, 1)
            transpose_norm(0, 1)

            def retention(h):
                first = type(h) is int and h == 0
                q = ret_q(h)
                u0, u1 = ret_uses(h)
                for c in range(12):
                    if first and c < 4:
                        pe.wait_ge(hT_done, c + 1)
                    in_chunk(q + c // 4, c, (0, 1, 0)[c // 4], (u0, u1, u0 + 1)[c // 4])
                    if first and c < 2:
                        transpose_norm(0, 2 + c)
                    if c == 0 and not first:
                        transpose_y(h - 1)
                    if c == 4:
                        pe.wait_ge(acc_free[0], u0 + 1)
                        if not first:
                            pe.wait_ge(side_read, side_reads(h))
                        transpose_tiles(stage, (0, 1)).then_inc(qkT_psum, 1)
                    if c == 5:
                        pe.wait_ge(qT_ready, h + 1)
                        pe.wait_ge(kT_ready, h + 1)
                        if not first:
                            pe.wait_ge(yT_done, h)
                        else:
                            pe.wait_ge(hT_done, CG)
                        for i in range(2):
                            pe.matmul(side[2][:, 0:2 * P], kT[:, i, 0:P], qT[:, i, :], start=(i == 0), stop=(i == 1))
                        for i in range(2):
                            ins = pe.matmul(side[2][:, 2 * P:3 * P], kT[:, i, P:2 * P], qT[:, i, P:2 * P], start=(i == 0), stop=(i == 1))
                        ins.then_inc(sT_psum, 1)
                    if c == 8:
                        pe.wait_ge(sT_ready, h + 1)
                        pe.wait_ge(acc_free[1], u1 + 1)
                        pe.matmul(side[0][:, :], sT[:, 0:P], v_sb[:, 0, :], start=True, stop=True)
                        pe.matmul(side[1][:, :], sT[:, P:2 * P], v_sb[:, 0, :], start=True, stop=False)
                        pe.matmul(side[1][:, :], sT[:, 2 * P:3 * P], v_sb[:, 1, :], start=False, stop=True).then_inc(o_psum, 1)
                if not first:
                    for j in range(CG):
                        if j == 0:
                            pe.wait_ge(yT_done, h)
                        if j < 3:
                            pair, uses = RET_OUT_PAIR[j], (u1 + 1, u0 + 2, u1 + 2)[j]
                            out_chunk(q + 3, j, pair, acc_free[pair], uses)
                        else:
                            out_chunk(q + 3, j, 2, side_read, side_reads(h) + 1)
                        if j == 2 and type(h) is int:
                            transpose_y(h)

            def transpose_y(h):
                pe.wait_ge(y_ready, h + 1)
                transpose_tiles(y_sb, (2, 3)).then_inc(yT_psum, 1)

            retention(0)
            with pe.Fori(1, H - 1) as h:
                retention(h)
            retention(H - 1)
            pe.wait_ge(yT_done, H)
            u0, u1 = RET_TAIL_USES
            for j in range(CG):
                out_chunk(RET_TAIL_Q, j, (j + 1) % 2, acc_free[(j + 1) % 2], (u1, u0, u1 + 1, u0 + 1)[j], *last_head_yT)
                if j == 1:
                    pe.wait_ge(side_read, 2 * H - 1)
                if j:
                    transpose_norm(1, j - 1)

            def transpose_q(g, in_stage):
                pe.wait_ge(*in_stage)
                if type(g) is int and g == 0:
                    pe.wait_ge(rawT_ready, 4)
                else:
                    pe.wait_ge(pT_ready, R * g)
                transpose_tiles(stage, (0, 1)).then_inc(qh_psum, 1)

            for c in range(4 * KV_GROUPS):
                i = c // 4
                if c < 4:
                    pe.wait_ge(hT_done, CG + c + 1)
                in_chunk(KV_Q + i, c, (i + 1) % 2, (KV_USES[1] + i // 2, KV_USES[0] + i // 2)[i % 2])
                if c == 0:
                    transpose_norm(1, 3)
                if c in (4, 8, 12, 20):
                    n = (4, 8, 12, 20).index(c)
                    before = c // 4 - 1
                    pe.wait_ge(acc_free[(before + 1) % 2], KV_USES[(before + 1) % 2] + before // 2 + 1)
                    if n == 0:
                        pe.wait_ge(hT_done, 2 * CG)
                    else:
                        pe.wait_ge(rawT_ready, n)
                    transpose_tiles(stage, (0, 1)).then_inc(rawT_psum, 1)
                if c in (5, 9):
                    n = c // 4 - 1
                    pe.wait_ge(window_ready, n + 1)
                    pe.wait_ge(w1_in, 32 + 16 * n)
                    for l in range(CMP_LEN):
                        ins = pe.matmul(side[2][:, 0:G * NC], w1[:, l, :], window[:, l, :], start=(l == 0), stop=(l == CMP_LEN - 1))
                    ins.then_inc(hid_psum, 1)
                if c in (6, 10):
                    n = c // 4 - 1
                    pe.wait_ge(hid_ready, n + 1)
                    pe.wait_ge(w2_in, 16 * n + 16)
                    if n == 0:
                        pe.matmul(side[3][:, 0:G * NC], w2[:, :], hidden[:, :], start=True, stop=True).then_inc(cmp_psum, 1)
                    else:
                        pe.wait_ge(cmp_ready, 1)
                        for g in range(G):
                            ins = pe.matmul(side[3][0:NC, g * DH:(g + 1) * DH], hidden[:, g * NC:(g + 1) * NC], w2[:, :], start=True, stop=True)
                        ins.then_inc(cmp_psum, 1)
                if c == 24:
                    transpose_q(0, (acc_free[0], KV_USES[0] + 3))
                if c == 25:
                    pe.wait_ge(gw_done, 1)
                    pe.wait_ge(acc_free[0], NSA_USES[0] - 1)
                    ghi = yT_hi[:, :, :].rearrange("p a b -> p (a b)")
                    glo = yT_lo[:, :, :].rearrange("p a b -> p (a b)")
                    for k in range(KT):
                        w = slice(k * NG, k * NG + P)
                        o = acc[0][0][:, 0:S]
                        pe.matmul(o, ghi[:, w], hT_hi[:, k, :], start=(k == 0), stop=False)
                        pe.matmul(o, ghi[:, w], hT_lo[:, k, :], start=False, stop=False)
                        ins = pe.matmul(o, glo[:, w], hT_hi[:, k, :], start=False, stop=(k == KT - 1))
                    ins.then_inc(gatesT_psum, 1)
                if c == 27:
                    pe.wait_ge(gatesT_ready, 1)
                    for t in range(TT):
                        ins = pe.transpose(acc[0][1][:, t * NG:(t + 1) * NG], gatesT[:, t * P:(t + 1) * P], ident[0:NG, 0:NG])
                    ins.then_inc(gates_psum, 1)

            def head_scores(g, r):
                u = R * g + r
                if type(u) is not int or u > 0:
                    pe.wait_ge(score_read, u)
                for b, (keysT, extra) in enumerate(((ksT, NC), (kwT, 0))):
                    keys = keysT[:, bass.ds(g, 1), :].rearrange("p a b -> p (a b)")
                    for t, (a, z) in enumerate(FULL):
                        ins = pe.matmul(side[2 + b][:, a - extra:z], qhT[:, r, t * P:(t + 1) * P], keys[:, 0:z - a + extra], start=True, stop=True)
                ins.then_inc(score_psum, 1)

            def transpose_probs(g, r):
                u = R * g + r
                pe.wait_ge(prob_ready, u + 1)
                if type(u) is not int or u > 0:
                    pe.wait_ge(pT_ready, u)
                if r and SLOTS[len(nsa_chunks(g))]["zT"] < SLOTS[len(nsa_chunks(g))]["probsT"][r]:
                    pe.wait_ge(zT_ready, g + 1)
                for b in range(2):
                    for i, at in enumerate((FULL[0][0], FULL[1][0], FULL[1][0] + P)):
                        pe.transpose(side[b][:, i * P:(i + 1) * P], prob[:, b, at:at + P], ident[:, :])
                    ins = pe.transpose(side[b][0:NC, 3 * P:4 * P], prob[:, 0, CMP_AT[b]:CMP_AT[b] + NC], ident[:, :])
                ins.then_inc(pT_psum, 1)

            def weighted_values(g):
                pe.wait_ge(pT_ready, R * g + R)
                pe.wait_ge(v_now_ready, g + 1)
                pe.wait_ge(score_read, R * g + R)
                for t, tiles in enumerate((((0, 0),), ((1, 0), (2, 1)))):
                    first = True
                    for b in range(2):
                        for tile, keys in tiles:
                            pe.matmul(side[2 + t][:, :], v_now[:, 2 * b + keys, :], pT[:, b, tile, :], start=first, stop=False)
                            first = False
                    ins = pe.matmul(side[2 + t][:, :], vc_now[:, :], pTc[0:NC, t, :], start=False, stop=True)
                ins.then_inc(pv_psum, 1)

            def transpose_z(g, heads):
                pe.wait_ge(acc_free[1], nsa_uses(g)[1] + 1)
                pe.wait_ge(pT_ready, R * g + heads)
                transpose_tiles(stage, (0, 1)).then_inc(zT_psum, 1)

            def sparse(g):
                q = nsa_q(g)
                u0, u1 = nsa_uses(g)
                kinds = nsa_chunks(g)
                at = SLOTS[len(kinds)]
                last = "q" not in kinds
                for c, kind in enumerate(kinds):
                    if kind == "z":
                        in_chunk(q, c, 1, u1)
                    elif kind == "q":
                        in_chunk(q + 1, c, 0, u0)
                    else:
                        j = c % 4
                        if j == 0:
                            pe.wait_ge(nsa_yT_done, TT * g)
                        out_chunk(q + c // 4, j, out_pair(g, j), acc_free[out_pair(g, j)], (u0, u1 + 1, u0 + 1, u1 + 2)[j] if last else (u1 + 1, u0 + 1, u1 + 2, u0 + 2)[j])
                    if c == 0:
                        pe.wait_ge(qh_ready, g + 1)
                        if type(g) is int and g == 0:
                            pe.wait_ge(late_in, 48)
                            pe.wait_ge(cmp_ready, 2)
                        else:
                            pe.wait_ge(y32_done, TT * g)
                    if c in at["probsT"]:
                        transpose_probs(g, at["probsT"].index(c))
                    if c in at["scores"]:
                        head_scores(g, at["scores"].index(c))
                    if c == at["zT"]:
                        transpose_z(g, sum(x <= c for x in at["probsT"]))
                    if c == at["qT"] and not last:
                        transpose_q(g + 1, (acc_free[0], u0 + 1))
                    if c == at["values"]:
                        weighted_values(g)

            sparse(0)
            with pe.Fori(1, G - 1) as g:
                sparse(g)
            sparse(G - 1)
            u0, u1 = NSA_TAIL_USES
            for j in range(CG):
                out_chunk(NSA_TAIL_Q, j, j % 2, acc_free[j % 2], (u0, u1, u0 + 1, u1 + 1)[j], *group_yT(G - 1), (nsa_yT_done, TT * G - 1) if j == 0 else None)


_INS = ["x", "norm_g", "ret_w_in", "ret_w_out", "nsa_w_in", "nsa_cmp_pos_k", "nsa_cmp_w1_k", "nsa_cmp_w2_k",
        "nsa_cmp_pos_v", "nsa_cmp_w1_v", "nsa_cmp_w2_v", "nsa_w_out", "final_g"]


def shape_constants(S, NC):
    import numpy as np
    p = np.arange(P)
    log_g = np.log1p(-np.exp2(-5.0 - np.arange(RET_HEADS)))
    diff = np.arange(2 * P)[None, :] - p[:, None]
    dk = 2048 // RET_HEADS
    dec = np.where(diff >= 0, np.exp(np.maximum(diff, 0)[None] * log_g[:, None, None]), 0.0) * dk ** -0.5
    slopes = -np.exp2(-8.0 * np.arange(1, NSA_HEADS + 1) / NSA_HEADS)
    far = 1e33

    def masked(d):
        return np.where(d >= 0, d, far)
    tile0 = p[:, None] - p[None, :]
    tile1 = P + p[:, None] - np.arange(2 * P)[None, :]
    ends = np.arange(NC) * CMP_STRIDE + CMP_LEN - 1
    cmp = [t * P + p[:, None] - ends[None, :] for t in range(2)]
    scores = [masked(d) for d in (cmp[0], tile0, cmp[1], tile1)]
    f = np.float32
    return {
        "identity": np.eye(P, dtype=f),
        "decay": np.ascontiguousarray(dec.transpose(1, 0, 2)).astype(f),
        "neg_slopes": np.broadcast_to(slopes, (P, NSA_HEADS)).astype(f),
        "distance": np.concatenate(scores, 1).astype(f),
        "cmp_seen": (p[:, None] >= CMP_LEN - 1).astype(f),
    }


def kernel(**inputs):
    import numpy as _np
    import concourse.bacc as _bacc
    from concourse import mybir as _mybir
    from concourse.bass_utils import run_bass_kernel_spmd as _run

    nc = _bacc.Bacc("TRN2", target_bir_lowering=False, num_devices=1)
    arrays, args = {}, []
    given = {name: _np.ascontiguousarray(inputs[name]) for name in _INS}
    S = given["x"].shape[1]
    given.update(shape_constants(S, (S - CMP_LEN) // CMP_STRIDE + 1))
    for name, a in given.items():
        arrays[f"in_{name}"] = a
        args.append(nc.dram_tensor(f"in_{name}", a.shape, _mybir.dt.from_np(a.dtype), kind="ExternalInput").ap())
    args.append(nc.dram_tensor("out_0", given["x"].shape, _mybir.dt.float32, kind="ExternalOutput").ap())
    trunk(nc, *args)
    r = _run(nc, [arrays], core_ids=[0])
    return r.results[0]["out_0"]
```

```python
from contextlib import ExitStack

import concourse.bass as bass
from concourse import mybir

F32 = mybir.dt.float32
F32R = mybir.dt.float32r
ACT = mybir.ActivationFunctionType
ALU = mybir.AluOpType
AX = mybir.AxisListType

P = 128
EPS = 1e-6
COLS = 512
KPC = 4
RING = 4
BRANCHES = 3
CMP_LEN, CMP_STRIDE = 32, 16
RET_HEADS = 8
NSA_HEADS = 16


def known(n, value):
    return type(n) is int and n == value


def trunk(nc, x, norm_g, ret_w_in, ret_w_out, nsa_w_in, cmp_pos_k, cmp_w1_k, cmp_w2_k, cmp_pos_v,
          cmp_w1_v, cmp_w2_v, nsa_w_out, final_g, identity, decay, neg_slopes, distance,
          cmp_seen, out):
    _, S, D = x.shape
    TT = S // P
    KT = D // P
    H = RET_HEADS
    DK = D // H
    G = NSA_HEADS // 4
    R = NSA_HEADS // G
    DH = D // NSA_HEADS
    KV = G * DH
    NC = (S - CMP_LEN) // CMP_STRIDE + 1
    NG = NSA_HEADS * BRANCHES
    GATE_COL = D + 6 * KV
    Z_COL = GATE_COL + NG
    CG = D // COLS
    FULL = [(NC, NC + P), (2 * NC + P, 2 * NC + 3 * P)]
    CMP_AT = [0, NC + P]
    SCORES = 2 * NC + 3 * P
    assert TT == 2 and DK == 256 and KV == COLS and R * DH == COLS and CG == RING == KPC == 4

    ret_in = ret_w_in[0].rearrange("(k p) n -> p k n", p=P)
    ret_out = ret_w_out[0].rearrange("(k p) n -> p k n", p=P)
    nsa_in = nsa_w_in[0].rearrange("(k p) n -> p k n", p=P)
    nsa_out = nsa_w_out[0].rearrange("(k p) n -> p k n", p=P)
    x_rows = x[0].rearrange("(t p) d -> p t d", p=P)
    out_rows = out[0].rearrange("(t p) d -> p t d", p=P)

    with ExitStack() as ctx:
        def sb(name, shape, dt=F32):
            return ctx.enter_context(nc.sbuf_tensor(name, shape, dt))

        def sem(name):
            return ctx.enter_context(nc.semaphore(name))

        w_raw = sb("w_raw", [P, RING, KPC, COLS])
        w_hi = sb("w_hi", [P, RING, KPC, COLS], F32R)
        w_lo = sb("w_lo", [P, RING, KPC, COLS], F32R)
        hT_hi = sb("hT_hi", [P, KT, S], F32R)
        hT_lo = sb("hT_lo", [P, KT, S], F32R)
        yT_hi = sb("yT_hi", [P, KPC, S], F32R)
        yT_lo = sb("yT_lo", [P, KPC, S], F32R)
        res = sb("res", [P, TT, D])
        stage = sb("stage", [P, TT, COLS])
        ksT = sb("ksT", [P, G, NC + S])
        kwT = sb("kwT", [P, G, S])
        vs = sb("vs", [P, TT, KV])
        vw = sb("vw", [P, TT, KV])
        ident = sb("ident", [P, P])
        dist = sb("dist", [P, SCORES])
        seen = sb("seen", [P, 1])
        slopes = sb("slopes", [P, NSA_HEADS])
        cols = sb("cols", [P, 96])
        gates = sb("gates", [P, TT, NG])
        vcmp = sb("vcmp", [NC, G * DH])
        sumsq = sb("sumsq", [P, TT, CG])
        meansq = sb("meansq", [P, TT])
        rstd = sb("rstd", [P, 3, TT])
        minus_half = sb("minus_half", [P, TT])
        bn6 = sb("bn6", [P, TT, 6])
        mv = sb("mv", [P, TT, 2])
        eps = sb("eps", [P, TT])
        head_rstd = sb("head_rstd", [P, TT])
        negmax = sb("negmax", [P, TT, BRANCHES])
        sums = sb("sums", [P, TT, BRANCHES])
        factor = sb("factor", [P, TT, BRANCHES])

        last_head_yT = hT_hi[:, KT - KPC:KT, :], hT_lo[:, KT - KPC:KT, :]
        last_group_yT = hT_hi[:, 0:KPC, :], hT_lo[:, 0:KPC, :]

        arena = sb("arena", [P, 7616])

        def piece(at, *dims):
            n = 1
            for d in dims:
                n *= d
            v = arena[:, at:at + n]
            if len(dims) == 2:
                v = v.rearrange("p (a b) -> p a b", a=dims[0])
            if len(dims) == 3:
                v = v.rearrange("p (a b c) -> p a b c", a=dims[0], b=dims[1])
            return v

        decays = piece(0, H, 2 * P)
        v_sb = piece(2048, TT, COLS)
        silu_gate = piece(3072, TT, COLS)
        y_sb = piece(4096, TT, COLS)
        qT = piece(5120, 2, S)
        kT = piece(5632, 2, S)
        sT = piece(6144, 3 * P)
        w1 = piece(0, CMP_LEN, DH)
        rawT = piece(4096, G, S)
        window = piece(5120, CMP_LEN, G * NC)
        vw_row = vw[:, :, :].rearrange("p t n -> p (t n)")
        gate_w = vw_row[:, 0:KT * NG].rearrange("p (k n) -> p k n", k=KT)
        w2 = vw_row[:, KT * NG:KT * NG + DH]
        hidden = vw_row[:, KT * NG + DH:KT * NG + DH + G * NC]
        pT = piece(0, 2, 3, R * P)
        pTc = piece(3072, TT, R * P)
        silu_zT = piece(4096, R, S)
        y32 = silu_zT
        qhT = piece(5120, R, S)
        prob = piece(6144, 2, SCORES)
        v_now = piece(6144 + 2 * SCORES, 4, P)
        gatesT = arena[0:NG, 0:S]
        vc_now = arena[0:NC, 7488:7488 + DH]
        final_gain = piece(0, D)
        gained = w_raw[:, :, 0:TT, :]

        pair_banks = [[ctx.enter_context(nc.psum_tensor(f"acc{a}{t}", [P, COLS], F32)) for t in range(TT)] for a in range(2)]
        side = [ctx.enter_context(nc.psum_tensor(f"side{i}", [P, COLS], F32)) for i in range(4)]
        acc = pair_banks + [side[0:2]]

        raw_in = [sem(f"raw_in{s}") for s in range(RING)]
        hi_done, lo_done = sem("hi_done"), sem("lo_done")
        first_hi, first_lo = sem("first_hi"), sem("first_lo")
        chunk_done = sem("chunk_done")
        acc_free = [sem("acc_free0"), sem("acc_free1")]
        x_in = [sem(f"x_in{j}") for j in range(CG)]
        ident_in, norm_g_in, pos_in, decays_in = sem("ident_in"), sem("norm_g_in"), sem("pos_in"), sem("decays_in")
        alibi_in = sem("alibi_in")
        w1_in, w2_in, gain_in = sem("w1_in"), sem("w2_in"), sem("gain_in")
        stored = sem("stored")
        cols_psum, cols_ready = sem("cols_psum"), sem("cols_ready")
        hT_psum, hT_hi_done, hT_done = sem("hT_psum"), sem("hT_hi_done"), sem("hT_done")
        squares_done, meansq_done, rstd_step, rstd_done = sem("squares_done"), sem("meansq_done"), sem("rstd_step"), sem("rstd_done")
        const_made, table_loaded = sem("const_made"), sem("table_loaded")
        qkT_psum, qT_ready, kT_ready = sem("qkT_psum"), sem("qT_ready"), sem("kT_ready")
        sT_psum, sT_ready, o_psum = sem("sT_psum"), sem("sT_ready"), sem("o_psum")
        stats_done, mv_done, head_rstd_step, head_rstd_done = sem("stats_done"), sem("mv_done"), sem("head_rstd_step"), sem("head_rstd_done")
        side_read = sem("side_read")
        y_ready = sem("y_ready")
        yT_psum, yT_hi_done, yT_done = sem("yT_psum"), sem("yT_hi_done"), sem("yT_done")
        rawT_psum, rawT_ready = sem("rawT_psum"), sem("rawT_ready")
        window_ready, hid_psum, hid_ready, cmp_psum, cmp_ready = sem("window_ready"), sem("hid_psum"), sem("hid_ready"), sem("cmp_psum"), sem("cmp_ready")
        gw_hi, gw_done, gates_psum, gates_ready = sem("gw_hi"), sem("gw_done"), sem("gates_psum"), sem("gates_ready")
        gatesT_psum, gatesT_ready = sem("gatesT_psum"), sem("gatesT_ready")
        qh_psum, qh_ready = sem("qh_psum"), sem("qh_ready")
        score_psum, score_read, negmax_ready, exp_done = sem("score_psum"), sem("score_read"), sem("negmax_ready"), sem("exp_done")
        recip_done, factor_done, prob_ready = sem("recip_done"), sem("factor_done"), sem("prob_ready")
        pT_psum, pT_ready, v_now_ready, pv_psum = sem("pT_psum"), sem("pT_ready"), sem("v_now_ready"), sem("pv_psum")
        zT_psum, zT_ready = sem("zT_psum"), sem("zT_ready")
        y32_done, nsa_hi_done, nsa_yT_done = sem("y32_done"), sem("nsa_hi_done"), sem("nsa_yT_done")
        last_tile0, last_added = sem("last_tile0"), sem("last_added")
        gained_done, final_dve, final_act = sem("gained_done"), sem("final_dve"), sem("final_act")

        RET_C = 16
        RET_OUT_PAIR = (1, 0, 1, 2)

        def ret_q(h):
            return 4 * h - 1 if not known(h, 0) else 0
        RET_TAIL_Q = 4 * H - 1
        KV_Q = RET_TAIL_Q + 1
        KV_COLS = [D + i * KV for i in range(4)] + [0, D + 4 * KV, D + 5 * KV]
        KV_GROUPS = len(KV_COLS)

        def nsa_q(g):
            return KV_Q + KV_GROUPS + 3 * g - (0 if known(g, 0) else 1)
        NSA_TAIL_Q = nsa_q(G - 1) + 2

        def nsa_chunks(g):
            return ["z"] * 4 + ([] if known(g, G - 1) else ["q"] * 4) + ([] if known(g, 0) else ["out"] * 4)

        def ret_uses(h):
            return (3 * h - 1, 3 * h - 2) if not known(h, 0) else (0, 0)
        RET_TAIL_USES = (3 * H - 1, 3 * H - 2)

        def side_reads(h):
            return 2 * h - 1

        KV_USES = (RET_TAIL_USES[0] + 2, RET_TAIL_USES[1] + 2)
        NSA_USES = (KV_USES[0] + 4, KV_USES[1] + 4)

        def nsa_uses(g):
            first = known(g, 0)
            return tuple(u if first else u + 3 * g - 2 for u in NSA_USES)

        SLOTS = {12: dict(scores=(1, 3, 5), factors=(2, 4, 6), probsT=(1, 3, 5, 7), zT=6, values=8, qT=9, next=10, next_factors=11),
                 8: dict(scores=(0, 2, 4), factors=(1, 3, 5), probsT=(0, 2, 4, 6), zT=5, values=7, qT=7, next=7, next_factors=8)}
        FIRST_SCORES = 4 * KV_GROUPS - 3
        NSA_TAIL_USES = (nsa_uses(G - 1)[0] + 2, nsa_uses(G - 1)[1] + 3)

        def out_pair(g, j):
            return j % 2 if known(g, G - 1) else (j + 1) % 2

        def out_projected(g):
            return chunk_done, 4 * nsa_q(g) + len(nsa_chunks(g))

        def group_yT(g):
            return last_group_yT if known(g, G - 1) else (yT_hi, yT_lo)

        def added(n, j):
            pair = (j + n) % 2
            return acc_free[pair], (RET_TAIL_USES if n == 1 else NSA_TAIL_USES)[pair] + j // 2 + 1

        block = ctx.enter_context(nc.Block())

        @block.sync
        def _(sp):
            def chunk(q, s, halves):
                if not known(q, 0):
                    sp.wait_ge(lo_done, 4 * q + s - 3)
                for to, src in halves:
                    sp.dma_start(to, src).then_inc(raw_in[s], 16)

            def by_rows(s, w, k0, col):
                return [(w_raw[:, s, 2 * i:2 * i + 2, :], w[:, bass.ds(k0 + 2 * i, 2), bass.ds(col, COLS)]) for i in range(2)]

            def by_columns(s, w, k0, col_a, col_b):
                return [(w_raw[:, s, :, i * DK:(i + 1) * DK], w[:, k0:k0 + KPC, bass.ds(c, DK)]) for i, c in enumerate((col_a, col_b))]

            def ret_inputs(h):
                q = ret_q(h)
                for c in range(12):
                    s = c % RING
                    if c < 4:
                        if known(h, 0):
                            sp.dma_start(res[:, :, s * COLS:(s + 1) * COLS], x_rows[:, :, s * COLS:(s + 1) * COLS]).then_inc(x_in[s], 16)
                        chunk(q, s, by_columns(s, ret_in, KPC * s, h * DK, D + h * DK))
                    elif c < 8:
                        chunk(q + 1, s, by_rows(s, ret_in, KPC * s, 2 * D + h * COLS))
                    else:
                        chunk(q + 2, s, by_rows(s, ret_in, KPC * s, 4 * D + h * COLS))

            def outputs(q, w, head):
                for j in range(CG):
                    chunk(q, j, by_rows(j, w, head * KPC, j * COLS))

            ret_inputs(0)
            with sp.Fori(1, H) as h:
                ret_inputs(h)
                outputs(ret_q(h) + 3, ret_out, h - 1)
            outputs(RET_TAIL_Q, ret_out, H - 1)
            for i, col in enumerate(KV_COLS):
                for s in range(RING):
                    chunk(KV_Q + i, s, by_rows(s, nsa_in, KPC * s, col))

            def sparse(g):
                for c, kind in enumerate(nsa_chunks(g)):
                    at, s = nsa_q(g) + c // RING, c % RING
                    if kind == "z":
                        chunk(at, s, by_rows(s, nsa_in, KPC * s, Z_COL + g * COLS))
                    elif kind == "q":
                        chunk(at, s, by_rows(s, nsa_in, KPC * s, g * COLS + COLS))
                    else:
                        chunk(at, s, by_rows(s, nsa_out, (g - 1) * KPC, s * COLS))

            sparse(0)
            with sp.Fori(1, G - 1) as g:
                sparse(g)
            sparse(G - 1)
            outputs(NSA_TAIL_Q, nsa_out, G - 1)
            for t in range(TT):
                for i in range(2):
                    sp.wait_ge((final_dve, final_act)[i], t + 1)
                    sp.dma_start(out_rows[:, t, :].rearrange("p (j n) -> p j n", j=CG)[:, 2 * i:2 * i + 2, :],
                                 gained[:, 2 * i:2 * i + 2, t, :]).then_inc(stored, 16)
            sp.wait_ge(stored, 16 * 2 * TT)

        @block.gpsimd
        def _(pool):
            pool.dma_start(stage[0:CMP_LEN, 1, 0:P], cmp_pos_k[0]).then_inc(pos_in, 16)
            pool.dma_start(stage[CMP_LEN:2 * CMP_LEN, 1, 0:P], cmp_pos_v[0]).then_inc(pos_in, 16)
            pool.memset(minus_half[:, :], -0.5).then_inc(const_made, 1)
            pool.wait_ge(x_in[CG - 1], 16)
            pool.dma_start(decays, decay).then_inc(decays_in, 16)
            pool.dma_start(slopes[:, :], neg_slopes).then_inc(alibi_in, 16)
            pool.dma_start(dist[:, :], distance).then_inc(alibi_in, 16)
            pool.dma_start(seen[:, :], cmp_seen).then_inc(alibi_in, 16)
            pool.wait_ge(const_made, 1)

            def token_factor(n, tiles, step):
                pool.wait_ge(meansq_done, step + 1)
                pool.tensor_scalar(meansq[:, tiles], meansq[:, tiles], 1.0 / D, EPS, ALU.mult, ALU.add).then_inc(rstd_step, 1)
                pool.wait_ge(rstd_step, step + 1)
                pool.tensor_tensor(rstd[:, n, tiles], meansq[:, tiles], minus_half[:, tiles], ALU.pow).then_inc(rstd_done, 1)

            def head_factor(h):
                pool.wait_ge(mv_done, TT * h + TT)
                pool.tensor_tensor(head_rstd[:, :], mv[:, :, 1], eps[:, :], ALU.add).then_inc(head_rstd_step, 1)
                pool.wait_ge(head_rstd_step, h + 1)
                pool.tensor_tensor(head_rstd[:, :], head_rstd[:, :], minus_half[:, :], ALU.pow).then_inc(head_rstd_done, 1)

            token_factor(0, slice(0, TT), 0)
            head_factor(0)
            with pool.Fori(1, H) as h:
                head_factor(h)
            pool.wait_ge(yT_done, H)
            pool.dma_start(w1, cmp_w1_k[0].rearrange("(l d) n -> d l n", d=DH)).then_inc(w1_in, 16)
            pool.dma_start(w2[:, :], cmp_w2_k[0]).then_inc(w2_in, 16)
            pool.dma_start(gate_w, nsa_in[:, :, GATE_COL:GATE_COL + NG]).then_inc(w1_in, 16)
            token_factor(1, slice(0, TT), 1)
            pool.wait_ge(hid_psum, 1)
            pool.dma_start(w1, cmp_w1_v[0].rearrange("(l d) n -> d l n", d=DH)).then_inc(w1_in, 16)
            pool.wait_ge(cmp_psum, 1)
            pool.dma_start(w2[:, :], cmp_w2_v[0]).then_inc(w2_in, 16)

            def group_values(g):
                if not known(g, 0):
                    pool.wait_ge(pv_psum, g)
                for b, v in enumerate((vs, vw)):
                    pool.tensor_copy(v_now[:, 2 * b:2 * b + 2, :], v[:, :, bass.ds(g * DH, DH)])
                pool.tensor_copy(vc_now[:, :], vcmp[:, bass.ds(g * DH, DH)]).then_inc(v_now_ready, 1)

            pool.wait_ge(gates_ready, 1)
            pool.wait_ge(cmp_ready, 2)
            group_values(0)
            with pool.Fori(1, G) as g:
                group_values(g)
            pool.wait_ge(pv_psum, G)
            pool.dma_start(final_gain, final_g.rearrange("(o d) -> o d", o=1).to_broadcast([P, D])).then_inc(gain_in, 16)
            for t in range(TT):
                token_factor(2, slice(t, t + 1), 2 + t)

        @block.scalar
        def _(act):
            def high(q, s):
                act.wait_ge(raw_in[s], 32 * q + 32)
                if not known(q, 0):
                    act.wait_ge(chunk_done, 4 * q + s - 3)
                act.copy(w_hi[:, s, :, :], w_raw[:, s, :, :]).then_inc(hi_done, 1)

            def ahead(q, c):
                high(q + (c + 2) // RING, (c + 2) % RING)

            def norm_high(layer, j):
                act.wait_ge(hT_psum, CG * layer + j + 1)
                if layer == 0 and j == 0:
                    act.wait_ge(cols_ready, 1)
                for i in range(KPC):
                    k = KPC * j + i
                    ins = act.activation(hT_hi[:, k, :], side[2 * (j % 2) + i // 2][:, (i % 2) * S:(i % 2 + 1) * S], ACT.Copy,
                                         scale=cols[:, KT * layer + k:KT * layer + k + 1])
                ins.then_inc(hT_hi_done, 1)

            def squares(n, j):
                if n == 0:
                    act.wait_ge(x_in[j], 16)
                    act.wait_ge(cols_psum, 2)
                else:
                    act.wait_ge(*added(n, j))
                if n or j:
                    act.wait_ge(squares_done, CG * n + j)
                for t in range(TT):
                    ins = act.activation(stage[:, t, :], res[:, t, j * COLS:(j + 1) * COLS], ACT.Square, accum_out=sumsq[:, t, j:j + 1])
                ins.then_inc(squares_done, 1)

            act.dma_start(ident[:, :], identity).then_inc(ident_in, 16)
            act.dma_start(stage[0:2 * KT, 0, 0:P], norm_g.rearrange("l (k p) -> (l k) p", p=P)).then_inc(norm_g_in, 16)
            act.wait_ge(const_made, 1)
            act.activation(eps[:, :], minus_half[:, :], ACT.Square).then_inc(table_loaded, 1)
            norm_high(0, 0)
            act.wait_ge(raw_in[0], 32)
            for i in range(2):
                act.copy(w_hi[:, 0, 2 * i:2 * i + 2, :], w_raw[:, 0, 2 * i:2 * i + 2, :]).then_inc((first_hi, hi_done)[i], 1)
            norm_high(0, 1)
            high(0, 1)
            squares(0, 0)
            squares(0, 1)

            def high_yT(h):
                act.wait_ge(yT_psum, h + 1)
                to = last_head_yT[0] if known(h, H - 1) else yT_hi
                for i in range(2):
                    act.copy(to[:, 2 * i:2 * i + 2, :], side[2 + i][:, :].rearrange("p (a b) -> p a b", a=2)).then_inc(yT_hi_done, 1)

            def retention(h):
                first = known(h, 0)
                q = ret_q(h)
                n0 = 4 * q
                for c in range(12 if first else RET_C):
                    ahead(q, c)
                    if first and c < 2:
                        norm_high(0, 2 + c)
                        squares(0, 2 + c)
                    if c == 4:
                        act.wait_ge(qkT_psum, h + 1)
                        act.copy(qT, side[0][:, :].rearrange("p (a b) -> p a b", a=2)).then_inc(qT_ready, 1)
                    if c == 7:
                        act.wait_ge(chunk_done, n0 + 8)
                        for t in range(TT):
                            ins = act.activation(v_sb[:, t, :], acc[1][t][:, :], ACT.Copy, scale=rstd[:, 0, t:t + 1])
                        ins.then_inc(acc_free[1], 1)
                    if c == 11:
                        act.wait_ge(chunk_done, n0 + 12)
                        for t in range(TT):
                            ins = act.activation(silu_gate[:, t, :], acc[0][t][:, :], ACT.Silu, scale=rstd[:, 0, t:t + 1])
                        ins.then_inc(acc_free[0], 1)
                    if c == (11 if first else 12):
                        act.wait_ge(side_read, 1 if first else side_reads(h) + 1)
                        act.wait_ge(head_rstd_done, h + 1)
                        for t in range(TT):
                            ins = act.activation(y_sb[:, t, :], y_sb[:, t, :], ACT.Copy, scale=head_rstd[:, t:t + 1])
                        ins.then_inc(y_ready, 1)
                    if c == 0 and not first:
                        high_yT(h - 1)
                    if c == 14 and known(h, H - 1):
                        high_yT(h)

            retention(0)
            with act.Fori(1, H - 1) as h:
                retention(h)
            retention(H - 1)
            for j in range(CG):
                ahead(RET_TAIL_Q, j)
                if j:
                    norm_high(1, j - 1)
                squares(1, j)

            def take_q(g):
                act.wait_ge(qh_psum, g + 1)
                for i in range(2):
                    ins = act.activation(qhT[:, 2 * i:2 * i + 2, :], side[i][:, :].rearrange("p (a b) -> p a b", a=2), ACT.Copy, scale=float(DH) ** -0.5)
                ins.then_inc(qh_ready, 1)

            def compress(n):
                act.wait_ge(hid_psum, n + 1)
                act.activation(hidden[:, :], side[2][:, 0:G * NC], ACT.Silu).then_inc(hid_ready, 1)

            def head_exps(g, r):
                u = R * g + r
                act.wait_ge(negmax_ready, u + 1)
                for b in range(2):
                    for t, (a, z) in enumerate(FULL):
                        act.activation(prob[:, b, a:z], prob[:, b, a:z], ACT.Exp, bias=negmax[:, t, b + 1:b + 2],
                                       accum_out=sums[:, t, b + 1:b + 2])
                for t, a in enumerate(CMP_AT):
                    ins = act.activation(prob[:, 0, a:a + NC], prob[:, 0, a:a + NC], ACT.Exp, bias=negmax[:, t, 0:1], accum_out=sums[:, t, 0:1])
                ins.then_inc(exp_done, 1)

            for c in range(4 * KV_GROUPS):
                ahead(KV_Q, c)
                if c == 0:
                    norm_high(1, 3)
                if c == 20:
                    take_q(0)
                if c in (4, 8, 12, 24):
                    n = (4, 8, 12, 24).index(c)
                    to = (rawT, rawT, ksT[:, :, NC:NC + S], kwT[:, :, :])[n]
                    act.wait_ge(rawT_psum, n + 1)
                    if n == 1:
                        act.wait_ge(window_ready, 1)
                    for i in range(2):
                        ins = act.copy(to[:, 2 * i:2 * i + 2, :], side[i][:, :].rearrange("p (a b) -> p a b", a=2))
                    ins.then_inc(rawT_ready, 1)
                if c in (5, 9):
                    compress(0 if c == 5 else 1)
                if c in (6, 10):
                    n = 0 if c == 6 else 1
                    act.wait_ge(cmp_psum, n + 1)
                    if n == 0:
                        act.copy(ksT[:, :, 0:NC], side[3][:, 0:G * NC].rearrange("p (g c) -> p g c", g=G)).then_inc(cmp_ready, 1)
                    else:
                        act.copy(vcmp[:, :], side[3][0:NC, :]).then_inc(cmp_ready, 1)
                if c == 16:
                    act.wait_ge(w1_in, 32)
                    act.copy(yT_hi[:, 0:3, :].rearrange("p a b -> p (a b)"), gate_w.rearrange("p a b -> p (a b)")).then_inc(gw_hi, 1)
                if c == 26:
                    act.wait_ge(gates_psum, 1)
                    for t in range(TT):
                        ins = act.activation(gates[:, t, :], acc[0][1][:, t * NG:(t + 1) * NG], ACT.Sigmoid, scale=rstd[:, 1, t:t + 1])
                    ins.then_inc(acc_free[0], 1)
                if c == FIRST_SCORES:
                    head_exps(0, 0)

            def take_pT(g, r):
                act.wait_ge(pT_psum, R * g + r + 1)
                for b in range(2):
                    act.copy(pT[:, b, :, r * P:(r + 1) * P], side[b][:, 0:3 * P].rearrange("p (a b) -> p a b", a=3))
                    ins = act.copy(pTc[0:NC, b, r * P:(r + 1) * P], side[b][0:NC, 3 * P:4 * P])
                ins.then_inc(pT_ready, 1)

            def take_z(q):
                act.wait_ge(chunk_done, 4 * q + 4)
                for t in range(TT):
                    ins = act.activation(stage[:, t, :], acc[1][t][:, :], ACT.Silu, scale=rstd[:, 1, t:t + 1])
                ins.then_inc(acc_free[1], 1)

            def take_zT(g):
                act.wait_ge(zT_psum, g + 1)
                for i in range(2):
                    ins = act.copy(silu_zT[:, 2 * i:2 * i + 2, :], side[i][:, :].rearrange("p (a b) -> p a b", a=2))
                ins.then_inc(zT_ready, 1)

            def high_y(g):
                if not known(g, 0) and not known(g, G - 1):
                    act.wait_ge(*out_projected(g))
                for t in range(TT):
                    tok = slice(t * P, (t + 1) * P)
                    act.wait_ge(y32_done, TT * g + t + 1)
                    act.copy(group_yT(g)[0][:, :, tok], y32[:, :, tok]).then_inc(nsa_hi_done, 1)

            def sparse(g):
                q = nsa_q(g)
                kinds = nsa_chunks(g)
                at = SLOTS[len(kinds)]
                for c, kind in enumerate(kinds):
                    ahead(q, c)
                    if c == 3:
                        take_z(q)
                    if c in at["probsT"]:
                        take_pT(g, at["probsT"].index(c))
                    if c in at["scores"]:
                        head_exps(g, at["scores"].index(c) + 1)
                    if c == at["zT"]:
                        take_zT(g)
                    if c == at["qT"] and "q" in kinds:
                        take_q(g + 1)
                    if c == at["next"] and "q" in kinds:
                        head_exps(g + 1, 0)
                high_y(g)

            sparse(0)
            with act.Fori(1, G - 1) as g:
                sparse(g)
            sparse(G - 1)
            for j in range(CG):
                if j < 2:
                    ahead(NSA_TAIL_Q, j)
                if j < CG - 1:
                    squares(2, j)
            for t in range(TT):
                act.wait_ge(last_added, t + 1)
                act.wait_ge(squares_done, CG * 3 - 1 + t)
                act.activation(stage[:, t, :], res[:, t, D - COLS:D], ACT.Square, accum_out=sumsq[:, t, CG - 1:CG]).then_inc(squares_done, 1)
                act.wait_ge(rstd_done, 3 + t)
                act.wait_ge(gained_done, CG + t)
                at = gained[:, 2:4, t, :]
                act.activation(at, at, ACT.Copy, scale=rstd[:, 2, t:t + 1]).then_inc(final_act, 1)

        @block.vector
        def _(dve):
            def low(q, s):
                dve.wait_ge(hi_done, 4 * q + s + 1)
                dve.tensor_tensor(w_lo[:, s, :, :], w_raw[:, s, :, :], w_hi[:, s, :, :].bitcast(F32), ALU.subtract).then_inc(lo_done, 1)

            def ahead(q, c):
                low(q + (c + 2) // RING, (c + 2) % RING)

            def norm_low(layer, j):
                dve.wait_ge(hT_hi_done, CG * layer + j + 1)
                for i in range(KPC):
                    k = KPC * j + i
                    ins = dve.scalar_tensor_tensor(out=hT_lo[:, k, :], in0=side[2 * (j % 2) + i // 2][:, (i % 2) * S:(i % 2 + 1) * S],
                                                   scalar=cols[:, KT * layer + k:KT * layer + k + 1], in1=hT_hi[:, k, :].bitcast(F32),
                                                   op0=ALU.mult, op1=ALU.subtract)
                ins.then_inc(hT_done, 1)

            def mean_square(n):
                dve.wait_ge(squares_done, CG * n + CG)
                if n:
                    dve.wait_ge(rstd_done, n)
                dve.tensor_reduce(meansq[:, :], sumsq[:, :, :], AX.X, ALU.add).then_inc(meansq_done, 1)

            def add_residual(chunk, pair, j):
                dve.wait_ge(chunk_done, chunk + 1)
                for t in range(TT):
                    at = res[:, t, j * COLS:(j + 1) * COLS]
                    ins = dve.tensor_tensor(at, acc[pair][t][:, :], at, ALU.add)
                ins.then_inc(acc_free[pair] if pair < 2 else side_read, 1)

            def take(chunk, pair, to, layer):
                dve.wait_ge(chunk_done, chunk)
                dve.wait_ge(rstd_done, layer + 1)
                for t in range(TT):
                    ins = dve.tensor_scalar(to[:, t, :], acc[pair][t][:, :], rstd[:, layer, t:t + 1], None, ALU.mult)
                ins.then_inc(acc_free[pair], 1)

            dve.wait_ge(cols_psum, 1)
            dve.tensor_copy(cols[:, 0:2 * KT], acc[1][0][:, 0:2 * KT]).then_inc(cols_ready, 1)
            dve.wait_ge(cols_ready, 1)
            norm_low(0, 0)
            for i in range(2):
                dve.wait_ge((first_hi, hi_done)[i], 1)
                half = slice(2 * i, 2 * i + 2)
                dve.tensor_tensor(w_lo[:, 0, half, :], w_raw[:, 0, half, :], w_hi[:, 0, half, :].bitcast(F32), ALU.subtract).then_inc((first_lo, lo_done)[i], 1)
            norm_low(0, 1)
            low(0, 1)
            dve.wait_ge(cols_psum, 2)
            dve.tensor_copy(cols[:, 2 * KT:96], acc[1][1][:, 0:2 * CMP_LEN]).then_inc(cols_ready, 1)

            def head_stats(h):
                dve.wait_ge(o_psum, h + 1)
                for t in range(TT):
                    dve.bn_stats(bn6[:, t, :], side[t][:, :]).then_inc(stats_done, 1)
                dve.wait_ge(stats_done, TT * h + TT)
                if known(h, 0):
                    dve.wait_ge(table_loaded, 1)
                dve.memset(eps[:, :], EPS)
                for t in range(TT):
                    dve.bn_aggr(mv[:, t, :], bn6[:, t, :]).then_inc(mv_done, 1)

            def head_y(h):
                dve.wait_ge(acc_free[0], ret_uses(h)[0] + 2)
                dve.wait_ge(mv_done, TT * h + TT)
                for t in range(TT):
                    ins = dve.scalar_tensor_tensor(out=y_sb[:, t, :], in0=side[t][:, :], scalar=mv[:, t, 0:1], in1=silu_gate[:, t, :],
                                                   op0=ALU.subtract, op1=ALU.mult)
                ins.then_inc(side_read, 1)

            def low_yT(h):
                hi, lo = last_head_yT if known(h, H - 1) else (yT_hi, yT_lo)
                for i in range(2):
                    dve.wait_ge(yT_hi_done, 2 * h + i + 1)
                    ins = dve.tensor_tensor(lo[:, 2 * i:2 * i + 2, :], side[2 + i][:, :].rearrange("p (a b) -> p a b", a=2),
                                            hi[:, 2 * i:2 * i + 2, :].bitcast(F32), ALU.subtract)
                ins.then_inc(yT_done, 1)

            def retention(h):
                first = known(h, 0)
                q = ret_q(h)
                for c in range(12 if first else RET_C):
                    ahead(q, c)
                    if first and c < 2:
                        norm_low(0, 2 + c)
                    if first and c == 1:
                        mean_square(0)
                    if c == 3:
                        take(4 * q + 4, 0, stage, 0)
                    if c == 4:
                        dve.wait_ge(qkT_psum, h + 1)
                        dve.tensor_copy(kT, side[1][:, :].rearrange("p (a b) -> p a b", a=2)).then_inc(kT_ready, 1)
                    if c == 5:
                        dve.wait_ge(sT_psum, h + 1)
                        if first:
                            dve.wait_ge(decays_in, 16)
                        mask = decays[:, bass.ds(h, 1), :].rearrange("p a b -> p (a b)")
                        dve.tensor_tensor(sT[:, 0:2 * P], side[2][:, 0:2 * P], mask, ALU.mult)
                        dve.tensor_tensor(sT[:, 2 * P:3 * P], side[2][:, 2 * P:3 * P], mask[:, 0:P], ALU.mult).then_inc(sT_ready, 1)
                    if c == 8:
                        head_stats(h)
                    if c >= 12:
                        add_residual(4 * q + c, RET_OUT_PAIR[c - 12], c - 12)
                    if c == (11 if first else 12):
                        head_y(h)
                    if c == 0 and not first:
                        low_yT(h - 1)
                    if c == 14 and known(h, H - 1):
                        low_yT(h)

            retention(0)
            with dve.Fori(1, H - 1) as h:
                retention(h)
            retention(H - 1)
            for j in range(CG):
                ahead(RET_TAIL_Q, j)
                add_residual(4 * RET_TAIL_Q + j, (j + 1) % 2, j)
                if j:
                    norm_low(1, j - 1)

            def make_window(n):
                dve.wait_ge(rawT_ready, n + 1)
                if n == 0:
                    dve.wait_ge(cols_ready, 2)
                if n:
                    dve.wait_ge(hid_psum, n)
                pos = cols[:, 2 * KT + CMP_LEN * n:2 * KT + CMP_LEN * (n + 1)]
                for g in range(G):
                    base = rawT[:, g, 0:CMP_LEN]
                    raw_at = bass.AP(base.tensor, base.offset, [base.ap[0], [1, CMP_LEN], [CMP_STRIDE, NC]])
                    pos_at = bass.AP(pos.tensor, pos.offset, [pos.ap[0], [1, CMP_LEN], [0, NC]])
                    ins = dve.tensor_tensor(window[:, :, g * NC:(g + 1) * NC], raw_at, pos_at, ALU.add)
                ins.then_inc(window_ready, 1)

            def head_scores(g, r):
                u = R * g + r
                dve.wait_ge(score_psum, u + 1)
                slope = slopes[:, bass.ds(g * R + r, 1)]
                dve.scalar_tensor_tensor(out=prob[:, 0, :], in0=dist[:, :], scalar=slope, in1=side[2][:, 0:SCORES], op0=ALU.mult, op1=ALU.add)
                for a, z in FULL:
                    ins = dve.scalar_tensor_tensor(out=prob[:, 1, a:z], in0=dist[:, a:z], scalar=slope, in1=side[3][:, a:z], op0=ALU.mult, op1=ALU.add)
                ins.then_inc(score_read, 1)
                dve.wait_ge(score_read, u + 1)
                for t, (a, z) in enumerate(FULL):
                    dve.tensor_reduce(negmax[:, t, 1:3], prob[:, :, a:z], AX.X, ALU.max, negate=True)
                for t, a in enumerate(CMP_AT):
                    ins = dve.tensor_reduce(negmax[:, t, 0:1], prob[:, 0, a:a + NC], AX.X, ALU.max, negate=True)
                ins.then_inc(negmax_ready, 1)

            def head_probs(g, r):
                u = R * g + r
                dve.wait_ge(exp_done, u + 1)
                dve.reciprocal(sums[:, :, :], sums[:, :, :]).then_inc(recip_done, 1)
                dve.wait_ge(recip_done, u + 1)
                dve.tensor_tensor(factor[:, :, :], sums[:, :, :], gates[:, :, bass.ds(g * R * BRANCHES + r * BRANCHES, BRANCHES)], ALU.mult).then_inc(factor_done, 1)
                dve.wait_ge(factor_done, u + 1)
                for b in range(2):
                    for t, (a, z) in enumerate(FULL):
                        dve.tensor_scalar(prob[:, b, a:z], prob[:, b, a:z], factor[:, t, b + 1:b + 2], None, ALU.mult)
                for t, a in enumerate(CMP_AT):
                    ins = dve.tensor_scalar(prob[:, 0, a:a + NC], prob[:, 0, a:a + NC], factor[:, t, 0:1], None, ALU.mult)
                ins.then_inc(prob_ready, 1)

            for c in range(4 * KV_GROUPS):
                n = 4 * KV_Q + c + 1
                if c == 27:
                    take(n, 1, vw, 1)
                ahead(KV_Q, c)
                if c == 0:
                    norm_low(1, 3)
                if c == 1:
                    mean_square(1)
                if c in (3, 7, 11, 19, 23):
                    take(n, (c // 4 + 1) % 2, stage, 1)
                if c in (4, 8):
                    make_window(c // 4 - 1)
                if c == 15:
                    take(n, 0, vs, 1)
                if c == 17:
                    dve.wait_ge(gw_hi, 1)
                    dve.tensor_tensor(yT_lo[:, 0:3, :].rearrange("p a b -> p (a b)"), gate_w.rearrange("p a b -> p (a b)"),
                                      yT_hi[:, 0:3, :].rearrange("p a b -> p (a b)").bitcast(F32), ALU.subtract).then_inc(gw_done, 1)
                if c == 25:
                    dve.wait_ge(gatesT_psum, 1)
                    dve.tensor_copy(gatesT, acc[0][0][0:NG, 0:S]).then_inc(gatesT_ready, 1)
                if c == FIRST_SCORES:
                    dve.wait_ge(alibi_in, 48)
                    head_scores(0, 0)
                if c == 27:
                    dve.wait_ge(acc_free[0], NSA_USES[0])
                    cmp_gates = gates[:, 0, 0:NG:BRANCHES]
                    dve.tensor_scalar(cmp_gates, cmp_gates, seen[:, 0:1], None, ALU.mult).then_inc(gates_ready, 1)
                    dve.wait_ge(gates_ready, 1)
                    head_probs(0, 0)

            def combine(g):
                dve.wait_ge(zT_ready, g + 1)
                dve.wait_ge(pv_psum, g + 1)
                for t in range(TT):
                    dve.tensor_tensor(y32[:, :, t * P:(t + 1) * P], side[2 + t][:, :].rearrange("p (a b) -> p a b", a=R),
                                      silu_zT[:, :, t * P:(t + 1) * P], ALU.mult).then_inc(y32_done, 1)

            def low_y(g):
                hi, lo = group_yT(g)
                for t in range(TT):
                    tok = slice(t * P, (t + 1) * P)
                    dve.wait_ge(nsa_hi_done, TT * g + t + 1)
                    dve.tensor_tensor(lo[:, :, tok], y32[:, :, tok], hi[:, :, tok].bitcast(F32), ALU.subtract).then_inc(nsa_yT_done, 1)

            def sparse(g):
                q = nsa_q(g)
                kinds = nsa_chunks(g)
                at = SLOTS[len(kinds)]
                for c, kind in enumerate(kinds):
                    if c in at["factors"]:
                        head_probs(g, at["factors"].index(c) + 1)
                    if c == at["next_factors"] and "q" in kinds:
                        head_probs(g + 1, 0)
                    ahead(q, c)
                    if c == at["values"]:
                        combine(g)
                        if "q" not in kinds:
                            low_y(g)
                    if kind == "out":
                        add_residual(4 * q + c, out_pair(g, c % 4), c % 4)
                    if c == 7 and "q" in kinds:
                        take(4 * q + 8, 0, stage, 1)
                    if c in at["scores"]:
                        head_scores(g, at["scores"].index(c) + 1)
                    if c == at["next"] and "q" in kinds:
                        head_scores(g + 1, 0)
                if "q" in kinds:
                    low_y(g)
                    if at["next_factors"] == len(kinds):
                        head_probs(g + 1, 0)

            sparse(0)
            with dve.Fori(1, G - 1) as g:
                sparse(g)
            sparse(G - 1)
            dve.wait_ge(gain_in, 16)
            for j in range(CG):
                if j < 2:
                    ahead(NSA_TAIL_Q, j)
                if j == CG - 1:
                    break
                add_residual(4 * NSA_TAIL_Q + j, j % 2, j)
                dve.wait_ge(*added(2, j))
                dve.wait_ge(lo_done, 4 * NSA_TAIL_Q + j + 1)
                for t in range(TT):
                    ins = dve.tensor_tensor(gained[:, j, t, :], res[:, t, j * COLS:(j + 1) * COLS], final_gain[:, j * COLS:(j + 1) * COLS], ALU.mult)
                ins.then_inc(gained_done, 1)
            last = slice(D - COLS, D)
            for t in range(TT):
                if t == 0:
                    dve.wait_ge(last_tile0, 1)
                    dve.wait_ge(lo_done, 4 * NSA_TAIL_Q + CG)
                else:
                    dve.wait_ge(chunk_done, 4 * NSA_TAIL_Q + CG)
                dve.tensor_tensor(res[:, t, last], acc[1][t][:, :], res[:, t, last], ALU.add).then_inc(last_added, 1)
                dve.wait_ge(last_added, t + 1)
                dve.tensor_tensor(gained[:, CG - 1, t, :], res[:, t, last], final_gain[:, last], ALU.mult).then_inc(gained_done, 1)
                dve.wait_ge(squares_done, CG * 3 + t)
                dve.wait_ge(rstd_done, 2 + t)
                dve.tensor_reduce(meansq[:, t:t + 1], sumsq[:, t:t + 1, :], AX.X, ALU.add).then_inc(meansq_done, 1)
                dve.wait_ge(rstd_done, 3 + t)
                at = gained[:, 0:2, t, :]
                dve.tensor_scalar(at, at, rstd[:, 2, t:t + 1], None, ALU.mult).then_inc(final_dve, 1)

        @block.tensor
        def _(pe):
            def chunk(q, s, xT_hi, xT_lo, k0, pair, start, stop, tile_ready=None, between=None, tile0_done=None):
                n = 4 * q + s
                by_halves = known(n, 0)
                pe.wait_ge(*((first_lo, 1) if by_halves else (lo_done, n + 1)))
                for t in range(TT):
                    if t == 1 and between:
                        between()
                    if tile_ready:
                        pe.wait_ge(tile_ready[0], tile_ready[1] + t)
                    tok = slice(t * P, (t + 1) * P)
                    for i in range(KPC):
                        a, z = start and i == 0, stop and i == KPC - 1
                        if by_halves and t == 0 and i == KPC // 2:
                            pe.wait_ge(lo_done, 1)
                        o = acc[pair][t][:, :]
                        pe.matmul(o, xT_hi[:, k0 + i, tok], w_hi[:, s, i, :], start=a, stop=False)
                        pe.matmul(o, xT_hi[:, k0 + i, tok], w_lo[:, s, i, :], start=False, stop=False)
                        ins = pe.matmul(o, xT_lo[:, k0 + i, tok], w_hi[:, s, i, :], start=False, stop=z)
                    if t == 0 and tile0_done:
                        ins.then_inc(tile0_done, 1)
                ins.then_inc(chunk_done, 1)

            def in_chunk(q, c, pair, uses, between=None):
                s = c % RING
                if s == 0 and not known(uses, 0):
                    pe.wait_ge(acc_free[pair], uses)
                chunk(q, s, hT_hi, hT_lo, KPC * s, pair, s == 0, s == RING - 1, None, between)

            def out_chunk(q, j, pair, free, uses, hi=yT_hi, lo=yT_lo, tile_ready=None, between=None, tile0_done=None):
                pe.wait_ge(free, uses)
                chunk(q, j, hi, lo, 0, pair, True, True, tile_ready, between, tile0_done)

            def transpose_norm(layer, j):
                if layer == 0:
                    pe.wait_ge(x_in[j], 16)
                else:
                    pe.wait_ge(*added(1, j))
                if j >= 2:
                    pe.wait_ge(hT_done, CG * layer + j - 1)
                for i in range(KPC):
                    k = KPC * j + i
                    for t in range(TT):
                        at = (i % 2) * S + t * P
                        ins = pe.transpose(side[2 * (j % 2) + i // 2][:, at:at + P], res[:, t, k * P:(k + 1) * P], ident[:, :])
                ins.then_inc(hT_psum, 1)

            def transpose_tiles(src, banks):
                for i in range(4):
                    for t in range(TT):
                        at = (i % 2) * S + t * P
                        ins = pe.transpose(side[banks[i // 2]][:, at:at + P], src[:, t, i * P:(i + 1) * P], ident[:, :])
                return ins

            pe.wait_ge(ident_in, 16)
            transpose_norm(0, 0)
            pe.wait_ge(norm_g_in, 16)                            
            pe.transpose(acc[1][0][:, 0:2 * KT], stage[0:2 * KT, 0, 0:P], ident[0:2 * KT, 0:2 * KT]).then_inc(cols_psum, 1)
            transpose_norm(0, 1)
            pe.wait_ge(pos_in, 32)
            pe.transpose(acc[1][1][:, 0:2 * CMP_LEN], stage[0:2 * CMP_LEN, 1, 0:P], ident[0:2 * CMP_LEN, 0:2 * CMP_LEN]).then_inc(cols_psum, 1)

            def retention(h):
                first = known(h, 0)
                q = ret_q(h)
                u0, u1 = ret_uses(h)
                for c in range(12):
                    if first and c < 4:
                        pe.wait_ge(hT_done, c + 1)
                    in_chunk(q + c // 4, c, (0, 1, 0)[c // 4], (u0, u1, u0 + 1)[c // 4])
                    if first and c < 2:
                        transpose_norm(0, 2 + c)
                    if c == 0 and not first:
                        transpose_y(h - 1)
                    if c == 4:
                        pe.wait_ge(acc_free[0], u0 + 1)
                        if not first:
                            pe.wait_ge(side_read, side_reads(h))
                        transpose_tiles(stage, (0, 1)).then_inc(qkT_psum, 1)
                    if c == 5:
                        pe.wait_ge(qT_ready, h + 1)
                        pe.wait_ge(kT_ready, h + 1)
                        if not first:
                            pe.wait_ge(yT_done, h)
                        else:
                            pe.wait_ge(hT_done, CG)
                        for i in range(2):
                            pe.matmul(side[2][:, 0:2 * P], kT[:, i, 0:P], qT[:, i, :], start=(i == 0), stop=(i == 1))
                        for i in range(2):
                            ins = pe.matmul(side[2][:, 2 * P:3 * P], kT[:, i, P:2 * P], qT[:, i, P:2 * P], start=(i == 0), stop=(i == 1))
                        ins.then_inc(sT_psum, 1)
                    if c == 8:
                        pe.wait_ge(sT_ready, h + 1)
                        pe.wait_ge(acc_free[1], u1 + 1)
                        pe.matmul(side[0][:, :], sT[:, 0:P], v_sb[:, 0, :], start=True, stop=True)
                        pe.matmul(side[1][:, :], sT[:, P:2 * P], v_sb[:, 0, :], start=True, stop=False)
                        pe.matmul(side[1][:, :], sT[:, 2 * P:3 * P], v_sb[:, 1, :], start=False, stop=True).then_inc(o_psum, 1)
                if not first:
                    for j in range(CG):
                        if j == 0:
                            pe.wait_ge(yT_done, h)
                        if j < 3:
                            pair, uses = RET_OUT_PAIR[j], (u1 + 1, u0 + 2, u1 + 2)[j]
                            out_chunk(q + 3, j, pair, acc_free[pair], uses)
                        else:
                            out_chunk(q + 3, j, 2, side_read, side_reads(h) + 1)
                        if j == 2 and known(h, H - 1):
                            transpose_y(h)

            def transpose_y(h):
                pe.wait_ge(y_ready, h + 1)
                transpose_tiles(y_sb, (2, 3)).then_inc(yT_psum, 1)

            retention(0)
            with pe.Fori(1, H - 1) as h:
                retention(h)
            retention(H - 1)
            pe.wait_ge(yT_done, H)
            u0, u1 = RET_TAIL_USES
            for j in range(CG):
                out_chunk(RET_TAIL_Q, j, (j + 1) % 2, acc_free[(j + 1) % 2], (u1, u0, u1 + 1, u0 + 1)[j], *last_head_yT)
                if j == 1:
                    pe.wait_ge(side_read, 2 * H - 1)
                if j:
                    transpose_norm(1, j - 1)

            def transpose_q(g, in_stage):
                pe.wait_ge(*in_stage)
                if known(g, 0):
                    pe.wait_ge(rawT_ready, 3)
                else:
                    pe.wait_ge(pT_ready, R * g)
                transpose_tiles(stage, (0, 1)).then_inc(qh_psum, 1)

            def head_scores(g, r):
                u = R * g + r
                if not known(u, 0):
                    pe.wait_ge(score_read, u)
                if r == 0:
                    pe.wait_ge(qh_ready, g + 1)
                    if known(g, 0):
                        pe.wait_ge(cmp_ready, 2)
                        pe.wait_ge(rawT_ready, 4)
                    else:
                        pe.wait_ge(y32_done, TT * g)
                for b, (keysT, extra) in enumerate(((ksT, NC), (kwT, 0))):
                    keys = keysT[:, bass.ds(g, 1), :].rearrange("p a b -> p (a b)")
                    for t, (a, z) in enumerate(FULL):
                        ins = pe.matmul(side[2 + b][:, a - extra:z], qhT[:, r, t * P:(t + 1) * P], keys[:, 0:z - a + extra], start=True, stop=True)
                ins.then_inc(score_psum, 1)

            for c in range(4 * KV_GROUPS):
                i = c // 4
                if c < 4:
                    pe.wait_ge(hT_done, CG + c + 1)
                in_chunk(KV_Q + i, c, (i + 1) % 2, (KV_USES[1] + i // 2, KV_USES[0] + i // 2)[i % 2])
                if c == 0:
                    transpose_norm(1, 3)
                if c in (4, 8, 12, 24):
                    n = (4, 8, 12, 24).index(c)
                    before = c // 4 - 1
                    pe.wait_ge(acc_free[(before + 1) % 2], KV_USES[(before + 1) % 2] + before // 2 + 1)
                    if n == 0:
                        pe.wait_ge(hT_done, 2 * CG)
                    elif n < 3:
                        pe.wait_ge(rawT_ready, n)
                    else:
                        pe.wait_ge(qh_ready, 1)
                    transpose_tiles(stage, (0, 1)).then_inc(rawT_psum, 1)
                if c in (5, 9):
                    n = c // 4 - 1
                    pe.wait_ge(window_ready, n + 1)
                    pe.wait_ge(w1_in, 32 + 16 * n)
                    for l in range(CMP_LEN):
                        ins = pe.matmul(side[2][:, 0:G * NC], w1[:, l, :], window[:, l, :], start=(l == 0), stop=(l == CMP_LEN - 1))
                    ins.then_inc(hid_psum, 1)
                if c in (6, 10):
                    n = c // 4 - 1
                    pe.wait_ge(hid_ready, n + 1)
                    pe.wait_ge(w2_in, 16 * n + 16)
                    if n == 0:
                        pe.matmul(side[3][:, 0:G * NC], w2[:, :], hidden[:, :], start=True, stop=True).then_inc(cmp_psum, 1)
                    else:
                        pe.wait_ge(cmp_ready, 1)
                        for g in range(G):
                            ins = pe.matmul(side[3][0:NC, g * DH:(g + 1) * DH], hidden[:, g * NC:(g + 1) * NC], w2[:, :], start=True, stop=True)
                        ins.then_inc(cmp_psum, 1)
                if c == 20:
                    transpose_q(0, (acc_free[1], KV_USES[1] + 3))
                if c == 24:
                    pe.wait_ge(gw_done, 1)
                    pe.wait_ge(acc_free[0], NSA_USES[0] - 1)
                    ghi = yT_hi[:, :, :].rearrange("p a b -> p (a b)")
                    glo = yT_lo[:, :, :].rearrange("p a b -> p (a b)")
                    for k in range(KT):
                        w = slice(k * NG, k * NG + P)
                        o = acc[0][0][:, 0:S]
                        pe.matmul(o, ghi[:, w], hT_hi[:, k, :], start=(k == 0), stop=False)
                        pe.matmul(o, ghi[:, w], hT_lo[:, k, :], start=False, stop=False)
                        ins = pe.matmul(o, glo[:, w], hT_hi[:, k, :], start=False, stop=(k == KT - 1))
                    ins.then_inc(gatesT_psum, 1)
                if c == 26:
                    pe.wait_ge(gatesT_ready, 1)
                    for t in range(TT):
                        ins = pe.transpose(acc[0][1][:, t * NG:(t + 1) * NG], gatesT[:, t * P:(t + 1) * P], ident[0:NG, 0:NG])
                    ins.then_inc(gates_psum, 1)
                if c == FIRST_SCORES:
                    head_scores(0, 0)

            def transpose_probs(g, r):
                u = R * g + r
                pe.wait_ge(prob_ready, u + 1)
                if not known(u, 0):
                    pe.wait_ge(pT_ready, u)
                if r and SLOTS[len(nsa_chunks(g))]["zT"] < SLOTS[len(nsa_chunks(g))]["probsT"][r]:
                    pe.wait_ge(zT_ready, g + 1)
                for b in range(2):
                    for i, at in enumerate((FULL[0][0], FULL[1][0], FULL[1][0] + P)):
                        pe.transpose(side[b][:, i * P:(i + 1) * P], prob[:, b, at:at + P], ident[:, :])
                    ins = pe.transpose(side[b][0:NC, 3 * P:4 * P], prob[:, 0, CMP_AT[b]:CMP_AT[b] + NC], ident[:, :])
                ins.then_inc(pT_psum, 1)

            def weighted_values(g):
                pe.wait_ge(pT_ready, R * g + R)
                pe.wait_ge(v_now_ready, g + 1)
                pe.wait_ge(score_read, R * g + R)
                for t, tiles in enumerate((((0, 0),), ((1, 0), (2, 1)))):
                    first = True
                    for b in range(2):
                        for tile, keys in tiles:
                            pe.matmul(side[2 + t][:, :], v_now[:, 2 * b + keys, :], pT[:, b, tile, :], start=first, stop=False)
                            first = False
                    ins = pe.matmul(side[2 + t][:, :], vc_now[:, :], pTc[0:NC, t, :], start=False, stop=True)
                ins.then_inc(pv_psum, 1)

            def transpose_z(g, heads):
                pe.wait_ge(acc_free[1], nsa_uses(g)[1] + 1)
                pe.wait_ge(pT_ready, R * g + heads)
                transpose_tiles(stage, (0, 1)).then_inc(zT_psum, 1)

            def sparse(g):
                q = nsa_q(g)
                u0, u1 = nsa_uses(g)
                kinds = nsa_chunks(g)
                at = SLOTS[len(kinds)]
                last = "q" not in kinds
                for c, kind in enumerate(kinds):
                    step = (lambda: weighted_values(g)) if c == at["values"] else None
                    if kind == "z":
                        in_chunk(q, c, 1, u1)
                    elif kind == "q":
                        in_chunk(q + 1, c, 0, u0, step)
                    else:
                        j = c % 4
                        uses = (u0, u1 + 1, u0 + 1, u1 + 2)[j] if last else (u1 + 1, u0 + 1, u1 + 2, u0 + 2)[j]
                        if j == 0:
                            pe.wait_ge(nsa_yT_done, TT * g)
                        out_chunk(q + c // 4, j, out_pair(g, j), acc_free[out_pair(g, j)], uses, between=step)
                    if c in at["probsT"]:
                        transpose_probs(g, at["probsT"].index(c))
                    if c in at["scores"]:
                        head_scores(g, at["scores"].index(c) + 1)
                    if c == at["zT"]:
                        transpose_z(g, sum(x <= c for x in at["probsT"]))
                    if c == at["qT"] and not last:
                        transpose_q(g + 1, (acc_free[0], u0 + 1))
                    if c == at["next"] and not last:
                        head_scores(g + 1, 0)

            sparse(0)
            with pe.Fori(1, G - 1) as g:
                sparse(g)
            sparse(G - 1)
            u0, u1 = NSA_TAIL_USES
            for j in range(CG):
                out_chunk(NSA_TAIL_Q, j, j % 2, acc_free[j % 2], (u0, u1, u0 + 1, u1 + 1)[j], *group_yT(G - 1), (nsa_yT_done, TT * G - 1) if j == 0 else None,
                          tile0_done=last_tile0 if j == CG - 1 else None)


_INS = ["x", "norm_g", "ret_w_in", "ret_w_out", "nsa_w_in", "nsa_cmp_pos_k", "nsa_cmp_w1_k", "nsa_cmp_w2_k",
        "nsa_cmp_pos_v", "nsa_cmp_w1_v", "nsa_cmp_w2_v", "nsa_w_out", "final_g"]


def shape_constants(S, NC):
    import numpy as np
    p = np.arange(P)
    log_g = np.log1p(-np.exp2(-5.0 - np.arange(RET_HEADS)))
    diff = np.arange(2 * P)[None, :] - p[:, None]
    dk = 2048 // RET_HEADS
    dec = np.where(diff >= 0, np.exp(np.maximum(diff, 0)[None] * log_g[:, None, None]), 0.0) * dk ** -0.5
    slopes = -np.exp2(-8.0 * np.arange(1, NSA_HEADS + 1) / NSA_HEADS)
    far = 1e33

    def masked(d):
        return np.where(d >= 0, d, far)
    tile0 = p[:, None] - p[None, :]
    tile1 = P + p[:, None] - np.arange(2 * P)[None, :]
    ends = np.arange(NC) * CMP_STRIDE + CMP_LEN - 1
    cmp = [t * P + p[:, None] - ends[None, :] for t in range(2)]
    scores = [masked(d) for d in (cmp[0], tile0, cmp[1], tile1)]
    f = np.float32
    return {
        "identity": np.eye(P, dtype=f),
        "decay": np.ascontiguousarray(dec.transpose(1, 0, 2)).astype(f),
        "neg_slopes": np.broadcast_to(slopes, (P, NSA_HEADS)).astype(f),
        "distance": np.concatenate(scores, 1).astype(f),
        "cmp_seen": (p[:, None] >= CMP_LEN - 1).astype(f),
    }


def kernel(**inputs):
    import numpy as _np
    import concourse.bacc as _bacc
    from concourse import mybir as _mybir
    from concourse.bass_utils import run_bass_kernel_spmd as _run

    nc = _bacc.Bacc("TRN2", target_bir_lowering=False, num_devices=1)
    arrays, args = {}, []
    given = {name: _np.ascontiguousarray(inputs[name]) for name in _INS}
    S = given["x"].shape[1]
    given.update(shape_constants(S, (S - CMP_LEN) // CMP_STRIDE + 1))
    for name, a in given.items():
        arrays[f"in_{name}"] = a
        args.append(nc.dram_tensor(f"in_{name}", a.shape, _mybir.dt.from_np(a.dtype), kind="ExternalInput").ap())
    args.append(nc.dram_tensor("out_0", given["x"].shape, _mybir.dt.float32, kind="ExternalOutput").ap())
    trunk(nc, *args)
    r = _run(nc, [arrays], core_ids=[0])
    return r.results[0]["out_0"]
```
